# Optimizing a Trainium2 kernel written in Bass

```python
import math
import jax, jax.numpy as jnp
from jax import lax
import numpy as np

D_MODEL = 1024
BATCH = 1
SEQ = 512
DEPTH = 2
DEC_BATCH = 8
DEC_SEQ = 8
PAST_LEN = 2048
PAGE_SIZE = 128

HEAD_DIM = 64
MIX_WIDTH = D_MODEL
NSA_HEADS = 8
NSA_KV_HEADS = 2
NSA_GROUP = NSA_HEADS // NSA_KV_HEADS
NSA_WIDTH = NSA_HEADS * HEAD_DIM
KV_W = NSA_KV_HEADS * HEAD_DIM
CONV_CH = MIX_WIDTH - NSA_WIDTH
N_BRANCH = 3
CMP_BLOCK = 32
CMP_STRIDE = 16
CMP_HIDDEN = 128
SEL_BLOCK = 64
N_SELECT = 16
WINDOW = 512
CONV_WIDTH = 31
D_FF = 2816
FFN_CONV_WIDTH = 3
ROPE_THETA = 10000.0
EPS = 1e-6
Q_BLOCK = 128
GATE_COLS = NSA_HEADS * N_BRANCH
IN_COLS = NSA_WIDTH + 6 * KV_W + GATE_COLS + 2 * CONV_CH

kernel_name = "hymba_nsa_conformer_convffn_step"

def rms_norm(x, g):
    xf = x.astype(jnp.float32)
    y = xf * lax.rsqrt(jnp.mean(xf * xf, -1, keepdims=True) + EPS)
    return (y * g.astype(jnp.float32)).astype(x.dtype)

def layer_norm(x, g, b):
    xf = x.astype(jnp.float32)
    mu = jnp.mean(xf, -1, keepdims=True)
    var = jnp.mean(jnp.square(xf - mu), -1, keepdims=True)
    y = (xf - mu) * lax.rsqrt(var + EPS) * g.astype(jnp.float32) + b.astype(jnp.float32)
    return y.astype(x.dtype)

def rope(x, pos):
    half = HEAD_DIM // 2
    inv = ROPE_THETA ** (-jnp.arange(half, dtype=jnp.float32) / half)
    ang = pos.astype(jnp.float32)[:, None] * inv[None, :]
    cos = jnp.cos(ang)[:, None, :]
    sin = jnp.sin(ang)[:, None, :]
    xf = x.astype(jnp.float32)
    x1, x2 = xf[..., :half], xf[..., half:]
    return jnp.concatenate([x1 * cos - x2 * sin, x2 * cos + x1 * sin], -1).astype(x.dtype)

def masked_softmax(s, mask):
    s = jnp.where(mask, s.astype(jnp.float32), -1e30)
    m = jnp.max(s, -1, keepdims=True)
    e = jnp.where(mask, jnp.exp(s - m), 0.0)
    return e / jnp.maximum(jnp.sum(e, -1, keepdims=True), 1e-30)

def dwconv_valid(xx, w):
    c = w.shape[1]
    return lax.conv_general_dilated(xx, w[:, None, :].astype(xx.dtype), (1,), "VALID",
                                    dimension_numbers=("NWC", "WIO", "NWC"), feature_group_count=c)

def in_projection(h, w_in, q_g, k_g, pos):
    B, S = h.shape[:2]
    z = h @ w_in
    q = z[..., :NSA_WIDTH].reshape(B, S, NSA_HEADS, HEAD_DIM)
    kv = z[..., NSA_WIDTH:NSA_WIDTH + 6 * KV_W].reshape(B, S, 6, NSA_KV_HEADS, HEAD_DIM)
    o = NSA_WIDTH + 6 * KV_W
    gates = jax.nn.sigmoid(z[..., o:o + GATE_COLS].astype(jnp.float32))
    gates = gates.reshape(B, S, NSA_KV_HEADS, NSA_GROUP, N_BRANCH).astype(h.dtype)
    glu = z[..., o + GATE_COLS:]
    u = glu[..., :CONV_CH] * jax.nn.sigmoid(glu[..., CONV_CH:])
    q = rope(rms_norm(q, q_g), pos).reshape(B, S, NSA_KV_HEADS, NSA_GROUP, HEAD_DIM)
    k_c = rope(rms_norm(kv[:, :, 0], k_g[0]), pos)
    k_s = rope(rms_norm(kv[:, :, 2], k_g[1]), pos)
    k_w = rope(rms_norm(kv[:, :, 4], k_g[2]), pos)
    return q, gates, k_c, kv[:, :, 1], k_s, kv[:, :, 3], k_w, kv[:, :, 5], u

def compress_rows(rows, pos_emb, w1, w2):
    B, L = rows.shape[:2]
    nc = (L - CMP_BLOCK) // CMP_STRIDE + 1
    idx = jnp.arange(nc)[:, None] * CMP_STRIDE + jnp.arange(CMP_BLOCK)[None, :]
    blk = rows[:, idx] + pos_emb[None, None, :, None, :]
    blk = jnp.swapaxes(blk, 2, 3).reshape(B, nc, NSA_KV_HEADS, CMP_BLOCK * HEAD_DIM)
    return jax.nn.gelu(blk @ w1) @ w2

def nsa_attend(q, qpos, gates, k_cmp, v_cmp, k_rows, v_rows, k_win, v_win, kwin_pos):
    B, QB = q.shape[:2]
    L = k_rows.shape[1]
    NC = k_cmp.shape[1]
    scale = HEAD_DIM ** -0.5
    s_c = jnp.einsum("bqkgd,bckd->bqkgc", q, k_cmp) * scale
    cmp_end = jnp.arange(NC) * CMP_STRIDE + (CMP_BLOCK - 1)
    p_c = masked_softmax(s_c, (cmp_end[None, :] <= qpos[:, None])[None, :, None, None, :])
    o_c = jnp.einsum("bqkgc,bckd->bqkgd", p_c.astype(v_cmp.dtype), v_cmp)
    nb = -(-L // SEL_BLOCK)
    c0 = jnp.arange(NC) * CMP_STRIDE
    s0 = jnp.arange(nb) * SEL_BLOCK
    overlap = jnp.clip(jnp.minimum(c0[:, None] + CMP_BLOCK, s0[None, :] + SEL_BLOCK)
                       - jnp.maximum(c0[:, None], s0[None, :]), 0, CMP_BLOCK).astype(jnp.float32) / CMP_BLOCK
    imp = jnp.einsum("bqkgc,cn->bqkn", p_c, overlap)
    blk = jnp.arange(nb)[None, :]
    cur = (qpos // SEL_BLOCK)[:, None]
    forced = (blk == 0) | (blk == cur) | (blk == cur - 1)
    visible = blk <= cur
    imp = jnp.where(forced[None, :, None, :], jnp.inf,
                    jnp.where(visible[None, :, None, :], imp, -jnp.inf))
    n_sel = min(N_SELECT, nb)
    _, sel = lax.top_k(imp, n_sel)
    tok = (sel[..., None] * SEL_BLOCK + jnp.arange(SEL_BLOCK)).reshape(B, QB, NSA_KV_HEADS, n_sel * SEL_BLOCK)
    tok_c = jnp.minimum(tok, L - 1)
    b_ix = jnp.arange(B)[:, None, None, None]
    h_ix = jnp.arange(NSA_KV_HEADS)[None, None, :, None]
    k_sel = k_rows[b_ix, tok_c, h_ix]
    v_sel = v_rows[b_ix, tok_c, h_ix]
    s_s = jnp.einsum("bqkgd,bqktd->bqkgt", q, k_sel) * scale
    p_s = masked_softmax(s_s, (tok <= qpos[None, :, None, None])[:, :, :, None, :])
    o_s = jnp.einsum("bqkgt,bqktd->bqkgd", p_s.astype(v_sel.dtype), v_sel)
    s_w = jnp.einsum("bqkgd,blkd->bqkgl", q, k_win) * scale
    dp = qpos[:, None] - kwin_pos[None, :]
    mask_w = (dp >= 0) & (dp < WINDOW) & (kwin_pos[None, :] >= 0)
    p_w = masked_softmax(s_w, mask_w[None, :, None, None, :])
    o_w = jnp.einsum("bqkgl,blkd->bqkgd", p_w.astype(v_win.dtype), v_win)
    o = gates[..., 0:1] * o_c + gates[..., 1:2] * o_s + gates[..., 2:3] * o_w
    return o.reshape(B, QB, NSA_WIDTH)

def nsa_prompt(q, gates, k_cmp, v_cmp, k_s, v_s, k_w, v_w):
    B, S = q.shape[:2]
    pad = jnp.zeros((B, WINDOW, NSA_KV_HEADS, HEAD_DIM), k_w.dtype)
    kw_pad = jnp.concatenate([pad, k_w], 1)
    vw_pad = jnp.concatenate([pad.astype(v_w.dtype), v_w], 1)

    def one_block(i):
        qs = i * Q_BLOCK
        qb = lax.dynamic_slice_in_dim(q, qs, Q_BLOCK, 1)
        gb = lax.dynamic_slice_in_dim(gates, qs, Q_BLOCK, 1)
        kwb = lax.dynamic_slice_in_dim(kw_pad, qs, WINDOW + Q_BLOCK, 1)
        vwb = lax.dynamic_slice_in_dim(vw_pad, qs, WINDOW + Q_BLOCK, 1)
        qpos = qs + jnp.arange(Q_BLOCK)
        kwpos = qs - WINDOW + jnp.arange(WINDOW + Q_BLOCK)
        return nsa_attend(qb, qpos, gb, k_cmp, v_cmp, k_s, v_s, kwb, vwb, kwpos)

    o = lax.map(one_block, jnp.arange(S // Q_BLOCK))
    return jnp.swapaxes(o, 0, 1).reshape(B, S, NSA_WIDTH)

def gather_pages(pool, page_table):
    g = pool[page_table]
    return g.reshape(page_table.shape[0], page_table.shape[1] * pool.shape[1], pool.shape[2], pool.shape[3])

def conformer_conv(u, buf, w, b, ln_g, ln_b):
    xx = jnp.concatenate([buf, u], 1)
    y = dwconv_valid(xx, w) + b
    y = jax.nn.silu(layer_norm(y, ln_g, ln_b))
    return y, xx[:, -(CONV_WIDTH - 1):]

def conv_ffn(h, buf, w_up, cw, cb, w_down):
    z = h @ w_up
    gate, up = z[..., :D_FF], z[..., D_FF:]
    gg = jnp.concatenate([buf, gate], 1)
    gc = dwconv_valid(gg, cw) + cb
    return (jax.nn.silu(gc) * up) @ w_down, gg[:, -(FFN_CONV_WIDTH - 1):]

def merge_and_ffn(x, o_nsa, u, conv_buf, ffn_buf, conv_w, conv_b, ln_g, ln_b, w_out, ffn_g, w_up, fcw, fcb, w_down):
    c, conv_state = conformer_conv(u, conv_buf, conv_w, conv_b, ln_g, ln_b)
    x = x + jnp.concatenate([o_nsa, c], -1) @ w_out
    f, ffn_state = conv_ffn(rms_norm(x, ffn_g), ffn_buf, w_up, fcw, fcb, w_down)
    return x + f, conv_state, ffn_state

def setup_inputs(seed: int = 0) -> dict:
    key = jax.random.key(seed)
    ks = jax.random.split(key, 40)
    n_pages = PAST_LEN // PAGE_SIZE
    n_pool = (DEC_BATCH * n_pages * 5) // 4
    win_buf = min(WINDOW, PAST_LEN)
    f32 = jnp.float32

    def nrm(k, shape, scale=1.0):
        return jax.random.normal(k, shape, f32) * scale

    pool_shape = (DEPTH, n_pool, PAGE_SIZE, NSA_KV_HEADS, HEAD_DIM)
    page_table = jax.random.permutation(ks[10], n_pool)[:DEC_BATCH * n_pages].reshape(DEC_BATCH, n_pages).astype(jnp.int32)
    return {
        "x_prompt": nrm(ks[0], (BATCH, SEQ, D_MODEL)),
        "x_sample": nrm(ks[1], (DEC_BATCH, DEC_SEQ, D_MODEL)),
        "cache_k_cmp": nrm(ks[2], pool_shape),
        "cache_v_cmp": nrm(ks[3], pool_shape),
        "cache_k_slc": nrm(ks[4], pool_shape),
        "cache_v_slc": nrm(ks[5], pool_shape),
        "state_k_win": nrm(ks[6], (DEPTH, DEC_BATCH, win_buf, NSA_KV_HEADS, HEAD_DIM)),
        "state_v_win": nrm(ks[7], (DEPTH, DEC_BATCH, win_buf, NSA_KV_HEADS, HEAD_DIM)),
        "state_conv": nrm(ks[8], (DEPTH, DEC_BATCH, CONV_WIDTH - 1, CONV_CH), 0.5),
        "state_ffn_conv": nrm(ks[9], (DEPTH, DEC_BATCH, FFN_CONV_WIDTH - 1, D_FF)),
        "page_table": page_table,
        "attn_norm": 1.0 + nrm(ks[11], (DEPTH, D_MODEL), 0.05),
        "w_in": nrm(ks[12], (DEPTH, D_MODEL, IN_COLS), D_MODEL ** -0.5),
        "q_norm": 1.0 + nrm(ks[13], (DEPTH, HEAD_DIM), 0.05),
        "k_norm": 1.0 + nrm(ks[14], (DEPTH, N_BRANCH, HEAD_DIM), 0.05),
        "kc_norm": 1.0 + nrm(ks[15], (DEPTH, HEAD_DIM), 0.05),
        "cmp_pos": nrm(ks[16], (DEPTH, CMP_BLOCK, HEAD_DIM), 0.1),
        "cmp_w1_k": nrm(ks[17], (DEPTH, CMP_BLOCK * HEAD_DIM, CMP_HIDDEN), (CMP_BLOCK * HEAD_DIM) ** -0.5),
        "cmp_w2_k": nrm(ks[18], (DEPTH, CMP_HIDDEN, HEAD_DIM), CMP_HIDDEN ** -0.5),
        "cmp_w1_v": nrm(ks[19], (DEPTH, CMP_BLOCK * HEAD_DIM, CMP_HIDDEN), (CMP_BLOCK * HEAD_DIM) ** -0.5),
        "cmp_w2_v": nrm(ks[20], (DEPTH, CMP_HIDDEN, HEAD_DIM), CMP_HIDDEN ** -0.5),
        "conv_w": nrm(ks[21], (DEPTH, CONV_WIDTH, CONV_CH), CONV_WIDTH ** -0.5),
        "conv_b": nrm(ks[22], (DEPTH, CONV_CH), 0.02),
        "conv_ln_g": 1.0 + nrm(ks[23], (DEPTH, CONV_CH), 0.05),
        "conv_ln_b": nrm(ks[24], (DEPTH, CONV_CH), 0.02),
        "w_out": nrm(ks[25], (DEPTH, MIX_WIDTH, D_MODEL), MIX_WIDTH ** -0.5),
        "ffn_norm": 1.0 + nrm(ks[26], (DEPTH, D_MODEL), 0.05),
        "w_up": nrm(ks[27], (DEPTH, D_MODEL, 2 * D_FF), D_MODEL ** -0.5),
        "ffn_conv_w": nrm(ks[28], (DEPTH, FFN_CONV_WIDTH, D_FF), FFN_CONV_WIDTH ** -0.5),
        "ffn_conv_b": nrm(ks[29], (DEPTH, D_FF), 0.02),
        "w_down": nrm(ks[30], (DEPTH, D_FF, D_MODEL), D_FF ** -0.5),
    }

def reference(x_prompt, x_sample, cache_k_cmp, cache_v_cmp, cache_k_slc, cache_v_slc,
              state_k_win, state_v_win, state_conv, state_ffn_conv, page_table,
              attn_norm, w_in, q_norm, k_norm, kc_norm, cmp_pos, cmp_w1_k, cmp_w2_k, cmp_w1_v, cmp_w2_v,
              conv_w, conv_b, conv_ln_g, conv_ln_b, w_out, ffn_norm, w_up, ffn_conv_w, ffn_conv_b, w_down):
    B, S = x_prompt.shape[:2]
    DB, DS = x_sample.shape[:2]
    past = page_table.shape[1] * cache_k_cmp.shape[2]
    win_buf = state_k_win.shape[2]
    pos_p = jnp.arange(S)
    pos_s = past + jnp.arange(DS)
    kwpos_s = past - win_buf + jnp.arange(win_buf + DS)
    p_win = min(WINDOW, S)
    y_p, y_s = x_prompt, x_sample
    pk_c, pv_c, pk_s, pv_s, pk_w, pv_w, p_cv, p_ff = [], [], [], [], [], [], [], []
    sk_c, sv_c, sk_s, sv_s, sk_w, sv_w, s_cv, s_ff = [], [], [], [], [], [], [], []
    for l in range(DEPTH):
        h = rms_norm(y_p, attn_norm[l])
        q, g, kc, vc, ksl, vsl, kw, vw, u = in_projection(h, w_in[l], q_norm[l], k_norm[l], pos_p)
        kcmp = rms_norm(compress_rows(kc, cmp_pos[l], cmp_w1_k[l], cmp_w2_k[l]), kc_norm[l])
        vcmp = compress_rows(vc, cmp_pos[l], cmp_w1_v[l], cmp_w2_v[l])
        o = nsa_prompt(q, g, kcmp, vcmp, ksl, vsl, kw, vw)
        conv0 = jnp.zeros((B, CONV_WIDTH - 1, CONV_CH), u.dtype)
        ffn0 = jnp.zeros((B, FFN_CONV_WIDTH - 1, D_FF), u.dtype)
        y_p, cv_state, ff_state = merge_and_ffn(y_p, o, u, conv0, ffn0, conv_w[l], conv_b[l], conv_ln_g[l], conv_ln_b[l],
                                                w_out[l], ffn_norm[l], w_up[l], ffn_conv_w[l], ffn_conv_b[l], w_down[l])
        pk_c.append(kc); pv_c.append(vc); pk_s.append(ksl); pv_s.append(vsl)
        pk_w.append(kw[:, -p_win:]); pv_w.append(vw[:, -p_win:]); p_cv.append(cv_state); p_ff.append(ff_state)

        h = rms_norm(y_s, attn_norm[l])
        q, g, kc, vc, ksl, vsl, kw, vw, u = in_projection(h, w_in[l], q_norm[l], k_norm[l], pos_s)
        kc_full = jnp.concatenate([gather_pages(cache_k_cmp[l], page_table), kc], 1)
        vc_full = jnp.concatenate([gather_pages(cache_v_cmp[l], page_table), vc], 1)
        ks_full = jnp.concatenate([gather_pages(cache_k_slc[l], page_table), ksl], 1)
        vs_full = jnp.concatenate([gather_pages(cache_v_slc[l], page_table), vsl], 1)
        kcmp = rms_norm(compress_rows(kc_full, cmp_pos[l], cmp_w1_k[l], cmp_w2_k[l]), kc_norm[l])
        vcmp = compress_rows(vc_full, cmp_pos[l], cmp_w1_v[l], cmp_w2_v[l])
        kw_full = jnp.concatenate([state_k_win[l], kw], 1)
        vw_full = jnp.concatenate([state_v_win[l], vw], 1)
        o = nsa_attend(q, pos_s, g, kcmp, vcmp, ks_full, vs_full, kw_full, vw_full, kwpos_s)
        y_s, cv_state, ff_state = merge_and_ffn(y_s, o, u, state_conv[l], state_ffn_conv[l], conv_w[l], conv_b[l],
                                                conv_ln_g[l], conv_ln_b[l], w_out[l], ffn_norm[l], w_up[l],
                                                ffn_conv_w[l], ffn_conv_b[l], w_down[l])
        sk_c.append(kc); sv_c.append(vc); sk_s.append(ksl); sv_s.append(vsl)
        sk_w.append(kw_full[:, -win_buf:]); sv_w.append(vw_full[:, -win_buf:]); s_cv.append(cv_state); s_ff.append(ff_state)
    st = jnp.stack
    return (y_p, y_s,
            st(pk_c), st(pv_c), st(pk_s), st(pv_s), st(pk_w), st(pv_w), st(p_cv), st(p_ff),
            st(sk_c), st(sv_c), st(sk_s), st(sv_s), st(sk_w), st(sv_w), st(s_cv), st(s_ff))


_drawn_inputs = setup_inputs


def setup_inputs(seed=0):
    import zlib

    import numpy as np

    out = dict(_drawn_inputs(seed))
    spreads = {}
    factors = {'cache_k_slc': 2.67,
     'q_norm': 8.0,
     'kc_norm': 8.0,
     'conv_ln_b': 4.557,
     'ffn_conv_b': 4.259}
    for name, (base, spread) in spreads.items():
        noise = np.random.default_rng([zlib.crc32(name.encode()), seed]).standard_normal(out[name].shape)
        drawn = base * np.exp(spread * noise) if base else spread * noise
        out[name] = __import__('jax').numpy.asarray(drawn.astype(out[name].dtype))
    for name, factor in factors.items():
        out[name] = (out[name] * factor).astype(out[name].dtype)
    return out
```

```python
from contextlib import ExitStack

import concourse.bass as bass
import numpy as np
from concourse import mybir

F32 = mybir.dt.float32
BF16 = mybir.dt.bfloat16
I32 = mybir.dt.int32
U32 = mybir.dt.uint32
ALU = mybir.AluOpType
ACT = mybir.ActivationFunctionType
X = mybir.AxisListType.X
ds = bass.ds

P = 128
DM, SEQ, DEPTH, DB, DS, PAST, PAGE = 1024, 512, 2, 8, 8, 2048, 128
HD, NH, NKV, G = 64, 8, 2, 4
CC = 512
DFF = 2816
WIN, CW, FW = 512, 31, 3
NSEL, SELB = 16, 64
CH = 128
EPS = 1e-6
SCALE = HD ** -0.5
NEG = -1e30
NS = DB * DS
NT = SEQ + NS
HN = NT // 2
KD = DM // P
CT = CC // P
FT = DFF // P
QKVC = NH * HD + 6 * NKV * HD + 3 * NH
NCH = 4
CHW = QKVC // NCH
TT = [(0, P), (1, P), (2, P), (3, P), (4, NS)]
NPOOL = DB * (PAST // PAGE) * 5 // 4
CHUNK = 16
NPAIR = CHUNK // 2
NCS = (PAST - 32) // CHUNK + 1
NCP = (SEQ - 32) // CHUNK + 1
NBLK = PAST // SELB
NCAND = NBLK - 2
NPICK = NSEL - 3
XSEG = CW - 1 + DS
XS0 = CW - 1 + SEQ
XW = XS0 + DB * XSEG
FSEG = FW - 1 + DS
FS0 = FW - 1 + SEQ
FWD = FS0 + DB * FSEG
FO_W = FWD - (FW - 1)
KVB = NH * HD
GB0 = KVB + 6 * P

DVE_STEPS, PU_STEPS, SB_STEPS, FF_STEPS = 533, 32, 25, 6

assert QKVC % NCH == 0 and NCS == 127 and NCP == 31


class Tally:

    def __init__(self, sem, per_layer, credit=0):
        self.sem, self.per, self.credit = sem, per_layer, credit

    def layer(self, l):
        self.base, self.n, self.stack = l * self.per + self.credit, 0, []
        return self

    def enter(self, i, per):
        self.stack.append((self.base, self.n, per))
        self.base, self.n = self.base + self.n + i * per, 0

    def leave(self, times):
        base, n, per = self.stack.pop()
        assert self.n == per, (self.sem.name, "in a loop", self.n, per)
        self.base, self.n = base, n + per * times

    def next(self, k=1):
        self.n += k
        return self.base + self.n

    def now(self):
        return self.base + self.n

    def end(self):
        assert self.n in (0, self.per), (self.sem.name, "in a layer", self.n, self.per)


def host_tables():
    f = np.float32
    half = HD // 2
    inv = (f(10000.0) ** (-np.arange(half, dtype=f) / f(half))).astype(f)
    pos = np.zeros((5, P), f)
    for t in range(4):
        pos[t] = t * P + np.arange(P)
    pos[4, :NS] = PAST + np.arange(NS) % DS
    ang = (pos[:, :, None] * inv[None, None, :]).astype(f)
    cs = np.stack([np.cos(ang), np.sin(ang)], 2).astype(f)
    rope = np.ascontiguousarray(cs.transpose(1, 0, 2, 3)).reshape(P, 5 * 2 * half)
    q = np.arange(P)
    causal = np.zeros((P, SEQ), f)
    causal[:, SEQ - P:] = np.where(q[None, :] <= q[:, None], 0, NEG)
    cmpm = np.zeros((P, 4, NCP), f)
    seen = np.ones((P, 4), f)
    for t in range(4):
        end = np.arange(NCP) * CHUNK + 31
        cmpm[:, t] = np.where(end[None, :] <= (t * P + q)[:, None], 0, NEG)
        seen[:, t] = (t * P + q) >= 31
    row = np.arange(64) % DS
    tok = (4 * np.arange(P)[None, :] + np.arange(4)[:, None]).reshape(-1)
    winm = np.where(tok[None, :] > row[:, None], 0, NEG).astype(f)
    newm = np.where(np.arange(DS)[None, :] <= row[:, None], 0, NEG).astype(f)
    c0 = np.arange(NCS) * CHUNK
    s0 = np.arange(NBLK) * SELB
    ov = np.clip(np.minimum(c0[:, None] + 32, s0[None, :] + SELB) - np.maximum(c0[:, None], s0[None, :]), 0, 32)
    ov = (ov / f(32)).astype(f)[:, 1:1 + NCAND]
    ov = np.concatenate([ov, np.zeros((1, NCAND), f)], 0)
    lower = np.tile((np.arange(NCAND)[None, :] < np.arange(NCAND)[:, None]).astype(f).reshape(1, -1), (64, 1))
    rr = np.arange(64)
    grp = ((rr[:, None] // 32 == rr[None, :] // 32) & (rr[:, None] % DS == rr[None, :] % DS)).astype(f)
    sub = (np.arange(P) % (PAGE // CHUNK)).astype(f).reshape(P, 1)
    return {"c_rope": rope, "c_causal": causal, "c_cmpm": cmpm.reshape(P, -1), "c_seen": seen,
            "c_ident": np.eye(P, dtype=f), "c_winm": winm, "c_newm": newm, "c_ov": ov, "c_lower": lower, "c_sub": sub, "c_grp": grp}


def build(nc, I, O):
    ctx = ExitStack()
    with ctx:
        def sb(name, shape, dt=F32):
            return ctx.enter_context(nc.sbuf_tensor(name, shape, dt))

        xT = sb("xT", [P, KD, NT])
        catT = sb("catT", [P, KD, NT])
        XC = sb("XC", [P, CT, XW])
        WR = sb("WR", [P, 4, KD, P])
        rA = sb("rA", [P, KD * NT])
        rB = sb("rB", [P, 2 * FT * P])
        rC = sb("rC", [P, FT * NT])
        rD = sb("rD", [P, 8192])
        ident = sb("ident", [P, P])
        ones = sb("ones", [P, P])
        causal = sb("causal", [P, SEQ])
        cmpm = sb("cmpm", [P, 4 * NCP])
        seen = sb("seen", [P, 4])
        winm = sb("winm", [64, WIN])
        newm = sb("newm", [64, DS])
        ov = sb("ov", [P, NCAND])
        lowf = rD[0:64, 0:NCAND * NCAND]
        lower = sb("lower", [64, NCAND * NCAND], BF16)
        grp = sb("grp", [64, 64])
        rope = sb("rope", [P, 5 * HD])
        PV = sb("PV", [P, 16 + CT * 34 + 16])
        FP = sb("FP", [P, FT * 20])
        Gn = sb("Gn", [P, 4 * HD])
        kcg = sb("kcg", [P, HD])
        w2 = sb("w2", [P, 2 * HD])
        posb = sb("posb", [P, 2])
        MS = sb("MS", [P, 5 * 14])
        RS = sb("RS", [P, 5 * 14])
        KM = sb("KM", [P, 4])
        nhalf = sb("nhalf", [P, 14])
        KcT = sb("KcT", [P, P])
        Vc = sb("Vc", [P, P])
        QBs = sb("QBs", [P, 64])
        GR = sb("GR", [64, DB * 3])
        st = sb("st", [P, 2 * 16])
        MX = sb("MX", [64, P + 64])
        impv = sb("impv", [64, 3 * NCAND])
        pgi = sb("pgi", [P, DB], I32)
        sub = sb("sub", [P, 1])
        idx = sb("idx", [P, DEPTH * DB], I32)
        idc = sb("idc", [P, 2], U32)
        PcT = sb("PcT", [P, 64])
        ps = ctx.enter_context(nc.psum_tensor("ps", [P, 8, 512], F32))

        hT = rA[:, :].rearrange("p (k n) -> p k n", k=KD)
        WD = rB[:, :].rearrange("p (s n) -> p s n", s=2)
        Z = rC[:, 0:5 * QKVC].rearrange("p (t c) -> p t c", t=5)
        o = 5 * QKVC
        QT = rC[:, o:o + G * NT].rearrange("p (g n) -> p g n", g=G)
        o += G * NT
        KT = rC[:, o:o + 2 * NT].rearrange("p (b n) -> p b n", b=2)
        o += 2 * NT
        XT = rC[:, o:o + 2048]
        CX = rC[:, o + 2048:o + 2048 + 254]
        CG = rC[:, o + 2302:o + 2302 + 254]
        KN = sb("KN", [P, P])
        lnsq = [rC[:, o + 576 * i:o + 576 * (i + 1)] for i in range(2)]
        lnmu = rC[:, o + 1152:o + 1728]
        lnrs = lnmu
        thl = [rC[:, 4096 + 576 * i:4672 + 576 * i] for i in range(2)]
        UX = rC[:, o + 2304:o + 2304 + CT * NS]
        QG = XT[:, 0:SEQ]
        KR = XC[:, :, :].rearrange("p c n -> p (c n)")[:, 0:2048]
        PTX = [KR[:, 0:512], KR[:, 512:1024]]
        DG = rD[:, 0:CW * P]
        KRs, XTs = [KR, rC[:, 0:2048]], [XT, rC[:, 2048:4096]]
        actT = rC[:, :].rearrange("p (f n) -> p f n", f=FT)
        xin = rC[:, 0:5 * DM].rearrange("p (t c) -> p t c", t=5)
        st1, st2 = rC[0:16, 0:128], rC[0:34, 128:640]
        st3, st4, st5 = rC[0:20, 640:3456], rC[0:120, 3456:4480], rC[0:16, 4480:4608]
        SQ = [rA[:, 896 * i:896 * (i + 1)] for i in range(2)]
        R1, R2 = rA[:, 1792:2688], rA[:, 2688:3584]
        UO = rA[:, 3584:4096].rearrange("p (c n) -> p c n", c=CT)
        US = rA[0:NS, 4096:4608].rearrange("p (c n) -> p c n", c=CT)
        PB = [rA[:, 1056 * i:1056 * (i + 1)] for i in range(2)]
        PT = [rA[:, 2112 + 1152 * i:2112 + 1152 * (i + 1)].rearrange("p (k n) -> p k n", k=9) for i in range(2)]
        S = rA[0:64, 0:2704]
        kwin, vwin, KwT = rA[:, 2704:3216], rA[:, 3216:3728], rA[:, 3728:4240]
        VN = rA[0:DS, 4240:4496]
        ksl, vsl = rB[:, 0:2048], rB[:, 2048:4096]
        PTS = rB[:, 4096:4096 + 23 * 64].rearrange("p (k n) -> p k n", k=23)
        kcv = [rD[:, 0:2048], rD[:, 2048:4096]]
        w1 = [rD[:, 4096 + 2048 * i:6144 + 2048 * i].rearrange("p (j m) -> p j m", j=16) for i in range(2)]
        sq2 = [rD[:, 576 * i:576 * (i + 1)] for i in range(2)]
        nrs = rD[:, 1152:1728]
        gth = [rD[:, 2304 + 576 * i:2880 + 576 * i] for i in range(2)]
        GBf = [rD[:, 594 * i:594 * (i + 1)] for i in range(2)]
        gcf = [rD[:, 1188 + 594 * i:1782 + 594 * i] for i in range(2)]
        thf = [rD[:, 2376 + 594 * i:2970 + 594 * i] for i in range(2)]
        upf = [rD[:, 3564 + 576 * i:4140 + 576 * i] for i in range(2)]
        FS = rD[:, 4716:4716 + FT * 18].rearrange("p (f n) -> p f n", f=FT)
        FO = rD[0:18, 5112:5112 + DFF]
        gates_dram = nc.dram_tensor("gates_scratch", (NS, 24), F32, kind="Internal").ap()

        PER = dict(
            layer_done=(1, 1), par_in=(16 * 14, 0), w1_in=(64, 0), par_made=(4, 0), par_kept=(4, 0),
            unit_made=(60, 4),
            z_made=(20, 0), z_kept=(20, 5), down_made=(8, 0),
            sq_made=(20, 0), sq_summed=(20, 0), mu_made=(1, 0), var_made=(3, 0), std_made=(3, 0), h_made=(16, 0),
            glu_gate=(4, 0), glu_done=(4, 2), conv_made=(3, 0), diag_made=(CW, 0), pe_conv_made=(1, 0), pe_conv_kept=(1, 0), mu_taken=(4, 0), ln_made=(4, 0), ln_tanh=(4, 0),
            conv_done=(4, 0), u_made=(2, 0), ux_made=(1, 0), kr_made=(16, 0), xz_made=(1, 0), u_kept=(2, 0), u_out=(32, 0),
            head_sq=(5, 0), head_ms=(5, 0), head_rs=(5, 0), qk_done=(5, 0), kv_out=(16 * 12, 0),
            gates_out=(16, 0), gates_in=(128, 0), tr_made=(10, 0), tr_kept=(10, 0), posb_made=(1, 0), posb_kept=(1, 0),
            kc_in=(8 * 16, 0), vc_in=(8 * 16, 0), xt_tr=(106, 0), xt_cp=(106, 0), hid_made=(18, 0), 
            cmp_in=(18, 0), cmp_th=(18, 0), cmp_g=(18, 0), cmp_out=(18, 0), kn_sq=(9, 0), kn_ms=(9, 0), kn_rs=(9, 0),
            kn_made=(9, 0), kct_made=(9, 0), kct_kept=(9, 0), vct_kept=(9, 0),
            qg_made=(4, 0), sc_made=(32, 1), masked=(32, 0), exped=(32, 0), p_ready=(32, 0), pt_made=(96, 6),
            pt_kept=(96, 2), o_made=(32, 0), o_kept=(32, 1),
            ks_in=(128, 0), vs_in=(128, 0), win_in=(8 * 64, 0), pv_done=(8, 1), qb_made=(8, 0), small_made=(8, 0),
            slc_made=(8, 1), win_made=(8, 1), cmp_max=(8, 0), cmp_exp=(8, 0), pc_ready=(8, 0), pct_made=(8, 0),
            pct_kept=(8, 0), imp_made=(8, 0), s_masked=(8, 1), s_exped=(8, 0), s_ready=(8, 0), st_made=(24, 0),
            st_kept=(24, 0), s_kept=(8, 1), x_upd=(16, 4), ff_kept=(44, 4), gb_ready=(22, 0), gc_done=(22, 0),
            fs_saved=(22, 2), ff_tanh=(22, 0), act_done=(22, 2), gb_zero=(1, 0), fo_made=(6, 0), fo_kept=(6, 0),
            fo_out=(32, 0), w_masked=(8, 0), dve_step=(DVE_STEPS, 0), pool_step=(16, 0),
            **{f"wr_in{s}": (16 * 2 + 48 * 2 + 16 * 11, 0) for s in range(4)},
            **{f"wd_in{s}": (16 * 6, 0) for s in range(2)})
        sh = {n: ctx.enter_context(nc.semaphore(n)) for n in
              list(PER) + ["const_in", "const_ok", "x_in", "xt_made", "xt_kept", "idx_made", "y_made", "y_kept",
                           "y_out", "bulk_out", "setup_step", "passed_pe", "passed_dve", "passed_pool"]}

        def counters(eng, l):
            T = {n: Tally(sh[n], *v) for n, v in PER.items()}
            for c in T.values():
                c.layer(l)

            def wait(name, k=1, less=0):
                eng.wait_ge(sh[name], T[name].next(k) - less)

            if eng is nc.gpsimd:
                def wait_alone(name, k=1, less=0):
                    wait(name, k, less)
                    alone(eng)
                return T, wait_alone
            return T, wait

        def alone(eng):
            eng.sem_inc(sh["passed_pe" if eng is nc.tensor else "passed_dve" if eng is nc.vector else "passed_pool"], 1)

        def pages(name):
            return I[name].rearrange("l n (c j) h d -> (l n c) (j h d)", j=CHUNK)

        def halves(ap):
            return ap.rearrange("p (a n) -> p a n", a=2)

        block = ctx.enter_context(nc.Block())

        @block.sync
        def _(sp):
            for dst, name in ((ident, "c_ident"), (rope, "c_rope"), (causal, "c_causal"), (cmpm, "c_cmpm"),
                              (seen, "c_seen"), (winm, "c_winm"), (newm, "c_newm"), (ov, "c_ov"), (sub, "c_sub"), (grp, "c_grp")):
                sp.dma_start(dst[:, :], I[name]).then_inc(sh["const_in"], 16)
            sp.dma_start(lowf, I["c_lower"]).then_inc(sh["const_in"], 16)
            for r in range(PAGE // CHUNK):
                sp.dma_start(pgi[r:P:PAGE // CHUNK, :], I["page_table"].rearrange("b m -> m b"), allow_slow_non_contiguous=True).then_inc(sh["const_in"], 16)
            for t in range(4):
                sp.dma_start(xin[:, t, :], I["x_prompt"][0, t * P:(t + 1) * P, :]).then_inc(sh["x_in"], 16)
            sp.dma_start(xin[0:NS, 4, :], I["x_sample"].rearrange("b s c -> (b s) c")).then_inc(sh["x_in"], 16)
            with sp.Fori(0, DEPTH) as l:
                T, wait = counters(sp, l)
                L = ds(l, 1)

                def W(name):
                    return I[name][L].rearrange("a r c -> (a r) c")

                def kpn(a):
                    return a.rearrange("(k p) n -> p k n", p=P)

                def par(dst, src):
                    sp.dma_start(dst, src).then_inc(sh["par_in"], 16)

                sp.wait_ge(sh["layer_done"], l + 1)
                par(st1[0:8], I["attn_norm"][L].rearrange("a (k p) -> (a k) p", p=P))
                par(st1[8:16], I["ffn_norm"][L].rearrange("a (k p) -> (a k) p", p=P))
                par(st2[0:CW], W("conv_w"))
                for n, name in enumerate(("conv_b", "conv_ln_g", "conv_ln_b")):
                    par(st2[CW + n:CW + n + 1], I[name][L])
                par(st3[0:FW], W("ffn_conv_w"))
                par(st3[FW:FW + 1], I["ffn_conv_b"][L])
                par(st3[FW + 1:20], I["state_ffn_conv"][L].rearrange("a b s c -> (a b s) c"))
                par(st4.rearrange("p (r c) -> p r c", r=2),
                    I["state_conv"][L].rearrange("a (r b) s c -> (a b s) r c", r=2))
                par(st5, I["cmp_pos"][L].rearrange("a (j q) d -> (a j) (q d)", q=2))
                par(Gn[:, 0:HD], I["q_norm"][L].rearrange("a d -> (a d)").partition_broadcast(P))
                par(Gn[:, HD:4 * HD], I["k_norm"][L].rearrange("a b d -> (a b d)").partition_broadcast(P))
                par(kcg[:, :], I["kc_norm"][L].rearrange("a d -> (a d)").partition_broadcast(P))

                def ring(s, *loads):
                    wait("unit_made", less=4)
                    for dst, src in loads:
                        sp.dma_start(dst, src).then_inc(sh[f"wr_in{s}"], 16)

                with sp.Fori(0, 2) as i:
                    T["unit_made"].enter(i, 4)
                    for s in range(4):
                        c0 = GB0 + 3 * NH + (s % 2) * CC + (i * 2 + s // 2) * P
                        ring(s, (WR[:, s], kpn(W("w_in")[:, ds(c0, P)])))
                    T["unit_made"].leave(2)
                for ch in range(NCH):
                    if ch >= 2:
                        wait("z_made", 5)
                    sp.dma_start(WD[:, ch % 2, 0:KD * CHW].rearrange("p (k n) -> p k n", k=KD),
                                 kpn(W("w_in")[:, ch * CHW:(ch + 1) * CHW])).then_inc(sh[f"wd_in{ch % 2}"], 16)
                with sp.Fori(0, 2) as i:
                    T["unit_made"].enter(i, 4)
                    for s in range(4):
                        cols = W("w_out")[:, ds((i * 4 + s) * P, P)]
                        ring(s, *[(WR[HD * h:HD * (h + 1), s, 0:G, :],
                                   cols[h * G * HD:(h + 1) * G * HD].rearrange("(g d) n -> d g n", g=G)) for h in range(2)],
                             (WR[:, s, G:KD, :], kpn(cols[NH * HD:DM])))
                    T["unit_made"].leave(2)

                def down(m, s):
                    sp.dma_start(WD[:, s].rearrange("p (f n) -> p f n", f=FT),
                                 W("w_down")[:, ds(m * P, P)].rearrange("(f p) n -> p f n", p=P)).then_inc(sh[f"wd_in{s}"], 16)

                wait("pv_done", 8)
                for s in range(2):
                    down(s, s)
                with sp.Fori(0, FT // 2) as i:
                    T["unit_made"].enter(i, 4)
                    for s in range(4):
                        c0 = (s % 2) * DFF + (i * 2 + s // 2) * P
                        ring(s, (WR[:, s], kpn(W("w_up")[:, ds(c0, P)])))
                    T["unit_made"].leave(FT // 2)
                with sp.Fori(0, 3) as i:
                    T["down_made"].enter(i, 2)
                    for s in range(2):
                        wait("down_made")
                        down(i * 2 + 2 + s, s)
                    T["down_made"].leave(3)
            for t, m in TT:
                sp.wait_ge(sh["y_kept"], 2 * (t + 1))
                dst = O["y_prompt"][0, t * P:(t + 1) * P, :] if t < 4 else O["y_sample"].rearrange("b s c -> (b s) c")
                sp.dma_start(dst, xin[0:m, t, :]).then_inc(sh["y_out"], 16)
            sp.wait_ge(sh["y_out"], 16 * 5)

        @block.gpsimd
        def _(pool):
            pool.memset(ones[:, :], 1.0).then_inc(sh["const_ok"], 1)
            pool.memset(nhalf[:, :], -0.5).then_inc(sh["const_ok"], 1)
            pool.memset(QBs[:, :], 0.0).then_inc(sh["const_ok"], 1)
            pool.wait_ge(sh["const_ok"], 3)
            for d, s in (("s_k_win", "state_k_win"), ("s_v_win", "state_v_win")):
                pool.dma_start(O[d].rearrange("l b w h d -> (l b) (w h d)")[:, 0:(WIN - DS) * P],
                               I[s].rearrange("l b w h d -> (l b) (w h d)")[:, DS * P:WIN * P]).then_inc(sh["bulk_out"], 16)
            pool.dma_start(O["s_conv"].rearrange("l b w c -> (l b) (w c)")[:, 0:(CW - 1 - DS) * CC],
                           I["state_conv"].rearrange("l b w c -> (l b) (w c)")[:, DS * CC:(CW - 1) * CC]).then_inc(sh["bulk_out"], 16)
            pool.wait_ge(sh["idx_made"], 1)
            with pool.Fori(0, DEPTH) as l:
                T, wait = counters(pool, l)
                L = ds(l, 1)
                pool.wait_ge(sh["layer_done"], l + 1)
                alone(pool)
                pool.memset(XC[:, :, 0:CW - 1], 0.0).then_inc(sh["xz_made"], 1)
                for n, name in enumerate(("cmp_w1_k", "cmp_w1_v")):
                    pool.dma_start(w1[n], I[name][L].rearrange("a r c -> (a r) c").rearrange("(j p) m -> p j m", p=P)).then_inc(sh["w1_in"], 16)
                for n, name in enumerate(("cmp_w2_k", "cmp_w2_v")):
                    pool.dma_start(w2[:, n * HD:(n + 1) * HD], I[name][L].rearrange("a r c -> (a r) c")).then_inc(sh["w1_in"], 16)
                pool.wait_ge(sh["glu_done"], l * 4 + 6)
                alone(pool)
                pool.tensor_copy(UX.rearrange("p (c b n) -> p c b n", c=CT, b=DB),
                                 XC[:, :, XS0:XW].rearrange("p c (b n) -> p c b n", b=DB)[:, :, :, CW - 1:XSEG]).then_inc(sh["ux_made"], 1)
                for t, m in TT:
                    wait("head_ms")
                    pool.tensor_tensor(RS[0:m, 14 * t:14 * t + 14], MS[0:m, 14 * t:14 * t + 14], nhalf[0:m, :],
                                       ALU.pow).then_inc(sh["head_rs"], 1)
                wait("u_kept", 2)
                pool.dma_start(O["p_conv"][L].rearrange("l a s c -> (l a s) c"),
                               UO[P - (CW - 1):P].rearrange("p c n -> p (c n)")).then_inc(sh["u_out"], 16)
                pool.dma_start(O["s_conv"][L, :, CW - 1 - DS:CW - 1, :].rearrange("l b s c -> (l b) s c"),
                               US.rearrange("p c n -> p (c n)")).then_inc(sh["u_out"], 16)
                def key_rsqrt(nb):
                    wait("kn_ms")
                    pool.tensor_tensor(KM[0:nb, 2:4], KM[0:nb, 0:2], nhalf[0:nb, 0:2], ALU.pow).then_inc(sh["kn_rs"], 1)

                def regroup(n):
                    src = kcv[n].rearrange("p (j q h d) -> p j q h d", j=NPAIR, q=2, h=2)
                    dst = KRs[n].rearrange("p (j h q d) -> p j h q d", j=NPAIR, h=2, q=2)
                    for h in range(2):
                        ins = pool.tensor_copy(dst[:, :, h], src[:, :, :, h])
                    ins.then_inc(sh["kr_made"], 1)

                def wait_at(name, value):
                    pool.wait_ge(sh[name], value)
                    alone(pool)

                def chunks_of(use, b):
                    pool.tensor_copy(idc[:, use:use + 1], idx[:, ds(l * DB + b, 1)]).then_inc(sh["pool_step"], 1)
                    wait("pool_step")
                    return bass.IndirectOffsetOnAxis(ap=idc[:, use:use + 1], axis=0)

                def gather_cmp(b, first=False):
                    off = chunks_of(0, b)
                    if not first:
                        wait_at("kr_made", T["kr_made"].now())
                    pool.indirect_dma_start(kcv[0], None, pages("cache_k_cmp"), off).then_inc(sh["kc_in"], 16)
                    pool.indirect_dma_start(kcv[1], None, pages("cache_v_cmp"), off).then_inc(sh["vc_in"], 16)

                gather_cmp(0, True)
                key_rsqrt(NCP)
                wait("qk_done", 5)
                order = ("k_cmp", "v_cmp", "k_slc", "v_slc", "k_win", "v_win")
                for n, name in enumerate(order):
                    pool.dma_start(O["p_" + name][L].rearrange("l a (t p) h d -> p (l a t) (h d)", p=P),
                                   Z[:, 0:4, KVB + n * P:KVB + (n + 1) * P]).then_inc(sh["kv_out"], 16)
                for n, name in enumerate(order):
                    src = Z[0:NS, 4, KVB + n * P:KVB + (n + 1) * P]
                    dst = O["s_" + name][L] if n < 4 else O["s_" + name][L, :, WIN - DS:WIN]
                    pool.dma_start(dst.rearrange("l b s h d -> (l b) s (h d)"), src).then_inc(sh["kv_out"], 16)
                pool.dma_start(gates_dram, Z[0:NS, 4, GB0:GB0 + 24]).then_inc(sh["gates_out"], 16)
                wait("gates_out", 16)
                for hg in range(8):
                    pool.dma_start(GR[hg * DS:(hg + 1) * DS, :].rearrange("i (b r) -> i b r", b=DB),
                                   gates_dram.rearrange("(b i) (k r) -> i b k r", i=DS, r=3)[:, :, hg, :]).then_inc(sh["gates_in"], 16)
                wait("kv_out", 16 * 12)
                wait("z_made", 20)
                wait("hid_made", 2)
                wait_at("o_kept", l * 32 + 33)

                def sequence(b, last):
                    off = chunks_of(1, b)
                    wait("slc_made", less=1)
                    pool.indirect_dma_start(ksl, None, pages("cache_k_slc"), off).then_inc(sh["ks_in"], 16)
                    wait("kc_in", 16)
                    wait_at("hid_made", T["hid_made"].now() - 1)
                    regroup(0)
                    wait("vc_in", 16)
                    wait_at("hid_made", T["hid_made"].now())
                    regroup(1)
                    T["hid_made"].next(2)
                    T["kr_made"].next(2)
                    if not last:
                        gather_cmp(b + 1)
                    wait("pv_done", less=1)
                    for dst, name in ((kwin, "state_k_win"), (vwin, "state_v_win")):
                        pool.dma_start(dst, I[name][L, ds(b, 1)].rearrange("l b (p j) h d -> (l b p) (j h d)", j=4)).then_inc(sh["win_in"], 16)
                    for n, name in enumerate(("s_v_slc", "s_v_win")):
                        src = O[name][L, ds(b, 1)] if n == 0 else O[name][L, ds(b, 1), WIN - DS:WIN]
                        pool.dma_start(VN[:, n * P:(n + 1) * P], src.rearrange("l b s h d -> (l b s) (h d)")).then_inc(sh["win_in"], 16)
                    pool.indirect_dma_start(vsl, None, pages("cache_v_slc"), off).then_inc(sh["vs_in"], 16)
                    key_rsqrt(NCS)
                    wait("ks_in", 16)
                    wait("vs_in", 16)

                with pool.Fori(0, DB - 1) as b:
                    per = dict(hid_made=2, slc_made=1, pv_done=1, kn_ms=1, pool_step=2, kc_in=16, vc_in=16, kr_made=2,
                               ks_in=16, vs_in=16)
                    for n, k in per.items():
                        T[n].enter(b, k)
                    sequence(b, False)
                    for n in per:
                        T[n].leave(DB - 1)
                sequence(DB - 1, True)
                wait("h_made", 16)
                for i in range(2):
                    ins = pool.memset(GBf[i][:, 0:FW - 1], 0.0)
                ins.then_inc(sh["gb_zero"], 1)
                with pool.Fori(0, FT // 2) as i:
                    T["gb_ready"].enter(i, 2)
                    for s in range(2):
                        wait("gb_ready")
                        pool.tensor_copy(FS[:, ds(i * 2 + s, 1), 0:2].rearrange("p a n -> p (a n)"), GBf[s][:, FS0 - 2:FS0])
                        pool.tensor_copy(FS[:, ds(i * 2 + s, 1), 2:18].rearrange("p a (b n) -> p (a b) n", b=DB),
                                         GBf[s][:, FS0:FWD].rearrange("p (b n) -> p b n", b=DB)[:, :, FSEG - 2:FSEG]).then_inc(sh["fs_saved"], 1)
                    T["gb_ready"].leave(FT // 2)
                wait("fo_kept", 6)
                pool.dma_start(O["p_ffn_conv"][L].rearrange("l a s c -> (l a s) c"), FO[0:2]).then_inc(sh["fo_out"], 16)
                pool.dma_start(O["s_ffn_conv"][L].rearrange("l b s c -> (l b s) c"), FO[2:18]).then_inc(sh["fo_out"], 16)
                wait("fo_out", 32)
                wait("u_out", 32)
            pool.wait_ge(sh["bulk_out"], 48)

        @block.tensor
        def _(pe):
            mm, tr = pe.matmul, pe.transpose
            pe.wait_ge(sh["const_in"], 16 * 19)
            pe.wait_ge(sh["const_ok"], 3)
            pe.wait_ge(sh["x_in"], 16 * 5)
            for t, m in TT:
                for hf in range(2):
                    n = 2 * t + hf
                    if n >= 8:
                        pe.wait_ge(sh["xt_kept"], n - 7)
                    for q in range(4):
                        ins = tr(ps[:, n % 8, q * m:(q + 1) * m], xin[0:m, t, (hf * 4 + q) * P:(hf * 4 + q + 1) * P], ident[0:m, 0:m])
                    ins.then_inc(sh["xt_made"], 1)
            with pe.Fori(0, DEPTH) as l:
                T, wait = counters(pe, l)
                wait("par_in", 16 * 14)
                alone(pe)
                tr(ps[:, 0, 0:16], st1, ident[0:16, 0:16])
                for c in range(CT):
                    tr(ps[:, 0, 16 + 34 * c:50 + 34 * c], st2[:, c * P:(c + 1) * P], ident[0:34, 0:34])
                tr(ps[:, 0, 152:168], st5, ident[0:16, 0:16]).then_inc(sh["par_made"], 1)
                for r in range(2):
                    for c in range(CT):
                        ins = tr(ps[:, 1 + r, c * 120:(c + 1) * 120], st4[:, r * CC + c * P:r * CC + (c + 1) * P], ident[0:120, 0:120])
                    ins.then_inc(sh["par_made"], 1)
                for f in range(FT):
                    ins = tr(ps[:, 3, f * 20:(f + 1) * 20], st3[:, f * P:(f + 1) * P], ident[0:20, 0:20])
                ins.then_inc(sh["par_made"], 1)

                def sums(bank, bufs, n):
                    for k in range(n):
                        wait("sq_made")
                        for hf in range(2):
                            ins = mm(ps[:, bank + hf, 0:HN], ones[:, :], bufs[k % 2][:, hf * HN:(hf + 1) * HN], start=k == 0, stop=k == n - 1)
                        ins.then_inc(sh["sq_summed"], 1)

                def unit(s, rhs, K=KD, w=None, bank=None):
                    bank = 2 * s if bank is None else bank
                    for k in range(K):
                        for hf in range(2):
                            ins = mm(ps[:, bank + hf, 0:HN], WR[:, s, k, :] if w is None else w[:, k * P:(k + 1) * P],
                                     rhs[:, k, hf * HN:(hf + 1) * HN], start=k == 0, stop=k == K - 1)
                    return ins

                sums(4, sq2, KD)
                wait("h_made", 8)
                alone(pe)
                with pe.Fori(0, 2) as i:
                    for n, k in (("unit_made", 4), ("glu_done", 2)) + tuple((f"wr_in{s}", 16) for s in range(4)):
                        T[n].enter(i, k)
                    for s in range(4):
                        wait(f"wr_in{s}", 16)
                        if s % 2 == 0:
                            wait("glu_done", less=2)
                        unit(s, hT).then_inc(sh["unit_made"], 1)
                    T["unit_made"].next(4)
                    for n in ("unit_made", "glu_done") + tuple(f"wr_in{s}" for s in range(4)):
                        T[n].leave(2)
                pe.wait_ge(sh["glu_done"], T["glu_done"].now())
                for ch in range(NCH):
                    wait(f"wd_in{ch % 2}", 16)
                    for t, m in TT:
                        wait("z_kept", less=5)
                        for k in range(KD):
                            ins = mm(ps[0:m, t, 0:CHW], hT[:, k, t * P:t * P + m], WD[:, ch % 2, k * CHW:(k + 1) * CHW],
                                     start=k == 0, stop=k == KD - 1)
                        ins.then_inc(sh["z_made"], 1)
                wait("w1_in", 64)
                wait("par_kept", 4)
                for n in range(2):
                    for j in range(16):
                        ins = mm(ps[:, 7, n:n + 1], w1[n][:, j, :], PV[:, 152 + j:153 + j], start=j == 0, stop=j == 15)
                ins.then_inc(sh["posb_made"], 1)
                pe.wait_ge(sh["z_kept"], T["z_kept"].now())
                pe.wait_ge(sh["glu_done"], l * 4 + 6)
                wait("xz_made")
                alone(pe)
                xs = XC[:, CT - 1, XS0:XW].rearrange("p (b n) -> p b n", b=DB)
                for k in range(CW):
                    wait("diag_made")
                    mm(ps[:, 0, :], DG[:, k * P:(k + 1) * P], XC[:, CT - 1, k:k + SEQ], start=k == 0, stop=k == CW - 1)
                    ins = mm(ps[:, 1, 0:NS].rearrange("p (b n) -> p b n", b=DB), DG[:, k * P:(k + 1) * P], xs[:, :, k:k + DS],
                             start=k == 0, stop=k == CW - 1)
                ins.then_inc(sh["pe_conv_made"], 1)
                for c in range(CT):
                    wait("conv_made" if c < CT - 1 else "pe_conv_kept")
                    for hf in range(2):
                        ins = mm(ps[:, 5 + hf, 0:HN], ones[:, :], catT[:, CT + c, hf * HN:(hf + 1) * HN], start=c == 0, stop=c == CT - 1)
                ins.then_inc(sh["mu_made"], 1)
                sums(5, lnsq, CT)
                wait("posb_kept")
                alone(pe)
                for c in range(CT):
                    ins = tr(ps[:, 7, c * P:(c + 1) * P], XC[:, c, XS0 - P:XS0], ident[:, :])
                ins.then_inc(sh["u_made"], 1)
                pe.wait_ge(sh["z_kept"], T["z_kept"].now())
                wait("ux_made")
                alone(pe)
                for c in range(CT):
                    ins = tr(ps[0:NS, 4, c * P:(c + 1) * P],
                             UX[:, c * NS:(c + 1) * NS], ident[:, :])
                ins.then_inc(sh["u_made"], 1)
                for t, m in TT:
                    wait("qk_done")
                    alone(pe)
                    for w in range(2):
                        n = 2 * t + w
                        if n >= 4:
                            wait("tr_kept")
                            alone(pe)
                        zt = Z[0:m, t, :]
                        for g in range(G if w == 0 else 2):
                            src = (zt[:, g * P:(g + 1) * P] if w == 0
                                   else zt[:, KVB + (2 + 2 * g) * P:KVB + (3 + 2 * g) * P])
                            ins = tr(ps[:, n % 4, g * m:(g + 1) * m], src, ident[0:m, 0:m])
                        ins.then_inc(sh["tr_made"], 1)
                wait("tr_kept", 4)
                alone(pe)
                for n in range(2):
                    for t in range(4):
                        ins = tr(ps[:, n, t * P:(t + 1) * P], Z[:, t, KVB + n * P:KVB + (n + 1) * P], ident[:, :])
                    ins.then_inc(sh["xt_tr"], 1)

                def turn_rows(n):
                    wait("kr_made")
                    alone(pe)
                    for a in range(16):
                        ins = tr(ps[:, a // 4, (a % 4) * P:(a % 4 + 1) * P], KRs[n][:, a * P:(a + 1) * P], ident[:, :])
                        if a % 4 == 3:
                            ins.then_inc(sh["xt_tr"], 1)

                def hidden(n, src, nb):
                    xt = src.rearrange("p (j h r) -> p j h r", j=NPAIR, h=2)
                    for j in range(16):
                        ins = mm(ps[:, 4, 0:2 * nb].rearrange("p (h r) -> p h r", h=2), w1[n][:, j, :],
                                 xt[:, j % NPAIR, :, j // NPAIR:j // NPAIR + nb], start=j == 0, stop=j == 15)
                    ins.then_inc(sh["hid_made"], 1)

                def second(n, nb):
                    for h in range(2):
                        ins = mm(ps[0:nb, 5 + n, h * HD:(h + 1) * HD], CG[:, h * nb:(h + 1) * nb], w2[:, n * HD:(n + 1) * HD], start=True, stop=True)
                    ins.then_inc(sh["cmp_out"], 1)

                def normed_keys(nb):
                    wait("kn_made")
                    alone(pe)
                    tr(ps[:, 6, 0:nb], KN[0:nb, :], ident[0:nb, 0:nb]).then_inc(sh["kct_made"], 1)
                    wait("kct_kept")
                    alone(pe)

                wait("u_kept", 2)
                wait("xt_cp")
                hidden(0, PTX[0], NCP)
                wait("cmp_g")
                second(0, NCP)
                wait("xt_cp")
                hidden(1, PTX[1], NCP)
                normed_keys(NCP)
                wait("cmp_g")
                second(1, NCP)
                wait("vct_kept")
                alone(pe)

                with pe.Fori(0, G) as g:
                    for n, k in (("qg_made", 1), ("masked", 8), ("p_ready", 8), ("pt_kept", 24), ("o_kept", 8)):
                        T[n].enter(g, k)
                    wait("qg_made")

                    def scores(u):
                        h, t = u // 4, u % 4
                        if u >= 1:
                            wait("masked")
                        n = (t + 1) * P
                        hp = slice(HD * h, HD * (h + 1))
                        q = QG[hp, t * P:(t + 1) * P]
                        mm(ps[:, u % 2, 0:n], q, KT[hp, 0, 0:n], start=True, stop=True)
                        mm(ps[:, 2 + u % 2, 0:n], q, KT[hp, 1, 0:n], start=True, stop=True)
                        mm(ps[:, 4, 64 * (u % 2):64 * (u % 2) + NCP], q, KcT[hp, 0:NCP], start=True, stop=True).then_inc(sh["sc_made"], 1)

                    def turn_p(u):
                        t = u % 4
                        pb = PB[u % 2]
                        wait("p_ready")
                        for e, (o, cnt) in enumerate(((0, t + 1), (512, t + 1), (1024, 1))):
                            pe.wait_ge(sh["pt_kept"], T["pt_kept"].now() + 3 * u + e + 1 - 2)
                            for k in range(cnt):
                                w = P if e < 2 else NCP
                                ins = tr(ps[0:w, 6 + (3 * u + e) % 2, k * P:(k + 1) * P], pb[:, o + k * P:o + k * P + w], ident[:, :])
                            ins.then_inc(sh["pt_made"], 1)

                    def weigh(u):
                        t = u % 4
                        pt = PT[u % 2]
                        pe.wait_ge(sh["pt_kept"], T["pt_kept"].now() + 3 * u + 3)
                        wait("o_kept", less=1)
                        out = ps[:, 5, (u % 2) * P:(u % 2 + 1) * P]
                        for k in range(t + 1):
                            mm(out, Z[:, k, KVB + 3 * P:KVB + 4 * P], pt[:, k, :], start=k == 0, stop=False)
                            mm(out, Z[:, k, KVB + 5 * P:KVB + 6 * P], pt[:, 4 + k, :], start=False, stop=False)
                        mm(out, Vc[0:NCP, :], pt[0:NCP, 8, :], start=False, stop=True).then_inc(sh["o_made"], 1)

                    scores(0)
                    scores(1)
                    for u in range(8):
                        turn_p(u)
                        if u:
                            weigh(u - 1)
                        if u + 2 < 8:
                            scores(u + 2)
                    weigh(7)
                    wait("masked")
                    T["pt_kept"].next(24)
                    for n in ("qg_made", "masked", "p_ready", "pt_kept", "o_kept"):
                        T[n].leave(G)
                pe.wait_ge(sh["o_kept"], T["o_kept"].now())
                alone(pe)

                with pe.Fori(0, DB) as b:
                    per = dict(kr_made=2, ks_in=16, vs_in=16, win_in=64, xt_cp=13, cmp_g=2, kn_made=1, kct_kept=1,
                               vct_kept=1, qb_made=1, pc_ready=1, pct_kept=1, s_ready=1, st_kept=3, s_masked=1, s_kept=1)
                    for n, k in per.items():
                        T[n].enter(b, k)
                    wait("s_masked", less=1)
                    wait("s_kept", less=1)

                    def turn_keys():
                        wait("ks_in", 16)
                        for j in range(16):
                            ins = tr(ps[:, j // 4, (j % 4) * P:(j % 4 + 1) * P], ksl[:, j * P:(j + 1) * P], ident[:, :])
                            if j % 4 == 3:
                                ins.then_inc(sh["xt_tr"], 1)
                        wait("win_in", 64)
                        for j in range(4):
                            ins = tr(ps[:, 7, j * P:(j + 1) * P], kwin[:, j * P:(j + 1) * P], ident[:, :])
                        ins.then_inc(sh["xt_tr"], 1)

                    turn_rows(0)
                    wait("xt_cp", 4)
                    turn_rows(1)
                    hidden(0, XTs[0], NCS)
                    wait("xt_cp", 4)
                    turn_keys()
                    wait("cmp_g")
                    second(0, NCS)
                    hidden(1, XTs[1], NCS)
                    normed_keys(NCS)
                    wait("qb_made")
                    rows = ps[0:64]
                    mm(rows[:, 5, 0:DS], QBs[:, :], KT[:, 0, ds(SEQ + b * DS, DS)], start=True, stop=True)
                    mm(rows[:, 5, DS:2 * DS], QBs[:, :], KT[:, 1, ds(SEQ + b * DS, DS)], start=True, stop=True)
                    mm(rows[:, 5, 16:16 + NCS], QBs[:, :], KcT[:, 0:NCS], start=True, stop=True).then_inc(sh["small_made"], 1)
                    wait("xt_cp", 5)
                    for n in range(4):
                        ins = mm(rows[:, n, :], QBs[:, :], XT[:, n * 512:(n + 1) * 512], start=True, stop=True)
                    ins.then_inc(sh["slc_made"], 1)
                    mm(rows[:, 7, :], QBs[:, :], KwT, start=True, stop=True).then_inc(sh["win_made"], 1)
                    wait("cmp_g")
                    second(1, NCS)
                    wait("vct_kept")
                    wait("pc_ready")
                    mm(ps[0:NCS, 6, 0:64], S[:, 2576:2576 + NCS], grp[:, :], start=True, stop=True).then_inc(sh["pct_made"], 1)
                    wait("pct_kept")
                    alone(pe)
                    mm(rows[:, 4, 0:NCAND], PcT[0:NCS, :], ov[0:NCS, :], start=True, stop=True).then_inc(sh["imp_made"], 1)
                    wait("s_ready")
                    alone(pe)
                    for e in range(3):
                        if e == 2:
                            wait("st_kept")
                            alone(pe)
                        for k in range(8 if e < 2 else 7):
                            j = 8 * e + k
                            o, w = ((j * P, P) if j < 16 else (2056 + (j - 16) * P, P) if j < 20
                                    else (2048, DS) if j == 20 else (2568, DS) if j == 21 else (2576, NCS))
                            ins = tr(ps[0:w, 6 + e % 2, k * 64:(k + 1) * 64], S[:, o:o + w], ident[0:64, 0:64])
                        ins.then_inc(sh["st_made"], 1)
                    wait("st_kept", 2)
                    wait("vs_in", 16)
                    out = ps[:, 4, 0:64]
                    for j in range(16):
                        mm(out, vsl[:, j * P:(j + 1) * P], PTS[:, j, :], start=j == 0, stop=False)
                    for j in range(4):
                        mm(out, vwin[:, j * P:(j + 1) * P], PTS[:, 16 + j, :], start=False, stop=False)
                    for n in range(2):
                        mm(out, VN[:, n * P:(n + 1) * P], PTS[0:DS, 20 + n, :], start=False, stop=False)
                    mm(out, Vc[0:NCS, :], PTS[0:NCS, 22, :], start=False, stop=True).then_inc(sh["pv_done"], 1)
                    for n in per:
                        T[n].leave(DB)
                pe.wait_ge(sh["s_kept"], T["s_kept"].now())
                wait("conv_done", 4)
                alone(pe)
                with pe.Fori(0, 2) as i:
                    for n, k in (("x_upd", 4),) + tuple((f"wr_in{s}", 48) for s in range(4)):
                        T[n].enter(i, k)
                    for s in range(4):
                        wait(f"wr_in{s}", 48)
                        wait("x_upd", less=4)
                        unit(s, catT).then_inc(sh["unit_made"], 1)
                    for n in ("x_upd",) + tuple(f"wr_in{s}" for s in range(4)):
                        T[n].leave(2)
                sums(4, sq2, KD)
                wait("h_made", 8)
                alone(pe)
                with pe.Fori(0, FT // 2) as i:
                    for n, k in (("ff_kept", 4),) + tuple((f"wr_in{s}", 16) for s in range(4)):
                        T[n].enter(i, k)
                    for s in range(4):
                        wait(f"wr_in{s}", 16)
                        wait("ff_kept", less=4)
                        unit(s, hT).then_inc(sh["unit_made"], 1)
                    for n in ("ff_kept",) + tuple(f"wr_in{s}" for s in range(4)):
                        T[n].leave(FT // 2)
                pe.wait_ge(sh["ff_kept"], T["ff_kept"].now())
                wait("fs_saved", 22)
                for e in range(6):
                    alone(pe)
                    if e >= 4:
                        wait("fo_kept")
                    for f in range(4 * e, min(4 * e + 4, FT)):
                        ins = tr(ps[0:18, 4 + e % 4, (f % 4) * P:(f % 4 + 1) * P], FS[:, f, :], ident[:, :])
                    ins.then_inc(sh["fo_made"], 1)
                wait("act_done", 22)
                alone(pe)
                with pe.Fori(0, 4) as i:
                    for n, k in (("x_upd", 2), ("wd_in0", 16), ("wd_in1", 16)):
                        T[n].enter(i, k)
                    for s in range(2):
                        wait(f"wd_in{s}", 16)
                        wait("x_upd", less=2)
                        unit(s, actT, FT, WD[:, s], 2 * s).then_inc(sh["down_made"], 1)
                    for n in ("x_upd", "wd_in0", "wd_in1"):
                        T[n].leave(4)
                T["fo_kept"].next(4)
            pe.wait_ge(sh["layer_done"], DEPTH + 1)
            for t, m in TT:
                for hf in range(2):
                    n = 2 * t + hf
                    if n >= 8:
                        pe.wait_ge(sh["y_kept"], n - 7)
                    for q in range(4):
                        ins = tr(ps[0:m, n % 8, q * P:(q + 1) * P], xT[:, hf * 4 + q, t * P:t * P + m], ident[:, :])
                    ins.then_inc(sh["y_made"], 1)

        @block.scalar
        def _(act):
            def copy(out, in_):
                return act.activation(out, in_, ACT.Copy)

            act.wait_ge(sh["idx_made"], 1)
            for t, m in TT:
                for hf in range(2):
                    n = 2 * t + hf
                    act.wait_ge(sh["xt_made"], n + 1)
                    copy(xT[:, 4 * hf:4 * hf + 4, t * P:t * P + m], ps[:, n % 8, 0:4 * m].rearrange("p (k n) -> p k n", k=4))\
                        .then_inc(sh["xt_kept" if n < 9 else "layer_done"], 1)
            with act.Fori(0, DEPTH) as l:
                T, wait = counters(act, l)
                act.wait_ge(sh["layer_done"], l + 1)
                wait("par_made")
                copy(PV[:, :], ps[:, 0, 0:168]).then_inc(sh["par_kept"], 1)
                for r in range(2):
                    wait("par_made")
                    for c in range(CT):
                        ins = copy(XC[:, c, XS0 + 4 * r * XSEG:XS0 + 4 * (r + 1) * XSEG].rearrange("p (b n) -> p b n", b=4)[:, :, 0:CW - 1],
                                   ps[:, 1 + r, c * 120:(c + 1) * 120].rearrange("p (b n) -> p b n", b=4))
                    ins.then_inc(sh["par_kept"], 1)
                wait("par_made")
                copy(FP[:, :], ps[:, 3, 0:440]).then_inc(sh["par_kept"], 1)

                def square(k, n0, buf, src):
                    if k >= 2:
                        wait("sq_summed")
                    act.activation(buf[k % 2], src, ACT.Square).then_inc(sh["sq_made"], 1)
                    if k == n0 - 1:
                        T["sq_summed"].next(2)

                def root(v):
                    wait("var_made")
                    act.activation(v, v, ACT.Sqrt).then_inc(sh["std_made"], 1)

                for k in range(KD):
                    square(k, KD, sq2, xT[:, k, :])
                root(nrs)
                with act.Fori(0, 2) as i:
                    for n, k in (("unit_made", 4), ("glu_done", 2)):
                        T[n].enter(i, k)
                    for s in (1, 3):
                        wait("unit_made", 2)
                        wait("glu_done", less=2)
                        act.activation(halves(gth[s // 2]), ps[:, 2 * s:2 * s + 2, 0:HN], ACT.Tanh, scale=0.5).then_inc(sh["glu_gate"], 1)
                    for n in ("unit_made", "glu_done"):
                        T[n].leave(2)
                for ch in range(NCH):
                    for t, m in TT:
                        wait("z_made")
                        copy(Z[0:m, t, ch * CHW:(ch + 1) * CHW], ps[0:m, t, 0:CHW]).then_inc(sh["z_kept"], 1)

                wait("posb_made")
                copy(posb[:, :], ps[:, 7, 0:2]).then_inc(sh["posb_kept"], 1)
                act.wait_ge(sh["posb_kept"], T["posb_kept"].next())

                def head_squares(t, m):
                    act.wait_ge(sh["z_kept"], T["z_kept"].base + 20)
                    act.wait_ge(sh["z_made"], T["z_made"].base + 20)
                    if t >= 2:
                        wait("qk_done")
                    zt = Z[0:m, t, :]
                    act.activation(zt[:, GB0:GB0 + 24], zt[:, GB0:GB0 + 24], ACT.Tanh, scale=0.5)
                    act.activation(SQ[t % 2][0:m, 0:512], zt[:, 0:512], ACT.Square)
                    act.activation(SQ[t % 2][0:m, 512:896].rearrange("p (j n) -> p j n", j=3),
                                   zt[:, KVB:KVB + 6 * P].rearrange("p (j x n) -> p j x n", j=3, x=2)[:, :, 0, :], ACT.Square).then_inc(sh["head_sq"], 1)

                act.wait_ge(sh["glu_done"], l * 4 + 6)
                wcol = 16 + 34 * (CT - 1)
                for k in range(CW):
                    act.activation(DG[:, k * P:(k + 1) * P], ident[:, :], ACT.Copy, scale=PV[:, wcol + k:wcol + k + 1]).then_inc(sh["diag_made"], 1)
                head_squares(*TT[0])
                head_squares(*TT[1])
                wait("pe_conv_made")
                act.activation(catT[:, KD - 1, 0:SEQ], ps[:, 0, :], ACT.Identity, bias=PV[:, wcol + CW:wcol + CW + 1])
                act.activation(catT[:, KD - 1, SEQ:NT], ps[:, 1, 0:NS], ACT.Identity, bias=PV[:, wcol + CW:wcol + CW + 1]).then_inc(sh["pe_conv_kept"], 1)
                head_squares(*TT[2])
                for c in range(CT):
                    wait("mu_taken")
                    square(c, CT, lnsq, catT[:, CT + c, :])
                head_squares(*TT[3])
                root(lnrs)
                head_squares(*TT[4])
                wait("u_made")
                copy(UO, ps[:, 7, :].rearrange("p (c n) -> p c n", c=CT)).then_inc(sh["u_kept"], 1)
                wait("u_made")
                copy(US, ps[0:NS, 4, :].rearrange("p (c n) -> p c n", c=CT)).then_inc(sh["u_kept"], 1)
                for t, m in TT:
                    wait("tr_made")
                    copy(QT[:, :, t * P:t * P + m], ps[:, (2 * t) % 4, 0:G * m].rearrange("p (g n) -> p g n", g=G)).then_inc(sh["tr_kept"], 1)
                    wait("tr_made")
                    copy(KT[:, :, t * P:t * P + m], ps[:, (2 * t + 1) % 4, 0:2 * m].rearrange("p (g n) -> p g n", g=2)).then_inc(sh["tr_kept"], 1)
                def turned(groups, to):
                    for q in range(groups):
                        wait("xt_tr")
                        copy(to[:, q * 512:(q + 1) * 512], ps[:, q, :]).then_inc(sh["xt_cp"], 1)

                def tanhed(nb):
                    wait("cmp_in")
                    act.activation(CG[:, 0:2 * nb], CG[:, 0:2 * nb], ACT.Tanh, scale=0.7978845608028654).then_inc(sh["cmp_th"], 1)

                def keys_kept(nb):
                    wait("cmp_out")
                    act.activation(KN[0:nb, :], ps[0:nb, 5, 0:P], ACT.Square).then_inc(sh["kn_sq"], 1)
                    wait("kct_made")
                    copy(KcT[:, 0:nb], ps[:, 6, 0:nb]).then_inc(sh["kct_kept"], 1)

                def values_kept(nb):
                    wait("cmp_out")
                    copy(Vc[0:nb, :], ps[0:nb, 6, 0:P]).then_inc(sh["vct_kept"], 1)

                for n in range(2):
                    wait("xt_tr")
                    to = PTX[n].rearrange("p (j h r) -> p j h r", j=NPAIR, h=2)
                    of = ps[:, n, :].rearrange("p (r j q) -> p j r q", j=NPAIR, q=2)
                    for q in range(2):
                        for h in range(2):
                            ins = copy(to[HD * q:HD * (q + 1), :, h], of[HD * h:HD * (h + 1), :, :, q])
                    ins.then_inc(sh["xt_cp"], 1)
                tanhed(NCP)
                keys_kept(NCP)
                tanhed(NCP)
                values_kept(NCP)
                T["hid_made"].next(2)
                wait("u_out", 32)
                with act.Fori(0, G) as g:
                    for n, k in (("masked", 8), ("pt_made", 24), ("o_made", 8)):
                        T[n].enter(g, k)

                    def exps(u):
                        t = u % 4
                        wait("masked")
                        c = 16 * (u % 2)
                        for e, (o, w) in enumerate(((1024, NCP), (0, (t + 1) * P), (512, (t + 1) * P))):
                            pb = PB[u % 2][:, o:o + w]
                            ins = act.activation(pb, pb, ACT.Exp, bias=st[:, c + 3 + e:c + 4 + e], scale=SCALE,
                                                 accum_out=st[:, c + 6 + e:c + 7 + e])
                        ins.then_inc(sh["exped"], 1)

                    def turned_p(u):
                        t = u % 4
                        for e, (o, cnt, w) in enumerate(((0, t + 1, P), (4, t + 1, P), (8, 1, NCP))):
                            wait("pt_made")
                            copy(PT[u % 2][0:w, o:o + cnt, :],
                                 ps[0:w, 6 + (3 * u + e) % 2, 0:cnt * P].rearrange("p (k n) -> p k n", n=P)).then_inc(sh["pt_kept"], 1)

                    def out_kept(u):
                        h, t = u // 4, u % 4
                        wait("o_made")
                        hp = slice(HD * h, HD * (h + 1))
                        copy(catT[hp, ds(g, 1), t * P:(t + 1) * P].rearrange("p a n -> p (a n)"), ps[hp, 5, (u % 2) * P:(u % 2 + 1) * P]).then_inc(sh["o_kept"], 1)

                    exps(0)
                    for u in range(8):
                        turned_p(u)
                        if u < 7:
                            exps(u + 1)
                        if u:
                            out_kept(u - 1)
                    out_kept(7)
                    for n in ("masked", "pt_made", "o_made"):
                        T[n].leave(G)
                wait("kv_out", 16 * 12)
                wait("gates_out", 16)
                for c in range(CT):
                    wait("ln_made")
                    if c >= 2:
                        wait("conv_done")
                    act.activation(thl[c % 2], catT[:, CT + c, :], ACT.Tanh, scale=0.5).then_inc(sh["ln_tanh"], 1)
                T["conv_done"].next(2)
                with act.Fori(0, DB) as b:
                    per = dict(slc_made=1, xt_tr=13, hid_made=2, cmp_out=2, cmp_in=2, kct_made=1, cmp_max=1, pct_made=1,
                               w_masked=1, s_masked=1, st_made=3, pv_done=1)
                    for n, k in per.items():
                        T[n].enter(b, k)
                    wait("slc_made", less=1)

                    turned(4, XTs[0])
                    turned(4, XTs[1])
                    wait("hid_made")
                    tanhed(NCS)
                    turned(4, XTs[0])
                    wait("xt_tr")
                    copy(KwT, ps[:, 7, :]).then_inc(sh["xt_cp"], 1)
                    keys_kept(NCS)
                    tanhed(NCS)
                    wait("cmp_max")
                    sc = S[:, 2576:2576 + NCS]
                    act.activation(sc, ps[0:64, 5, 16:16 + NCS], ACT.Exp, bias=st[0:64, 1:2], scale=SCALE, accum_out=st[0:64, 2:3]).then_inc(sh["cmp_exp"], 1)
                    values_kept(NCS)
                    T["hid_made"].next()
                    wait("pct_made")
                    copy(PcT[0:NCS, :], ps[0:NCS, 6, 0:64]).then_inc(sh["pct_kept"], 1)
                    wait("w_masked")
                    act.activation(S[:, 2056:2576], S[:, 2056:2576], ACT.Exp, bias=st[0:64, 15:16], scale=SCALE, accum_out=st[0:64, 17:18])
                    wait("s_masked")
                    act.activation(S[:, 0:2056], S[:, 0:2056], ACT.Exp, bias=st[0:64, 14:15], scale=SCALE, accum_out=st[0:64, 16:17]).then_inc(sh["s_exped"], 1)
                    for e in range(3):
                        wait("st_made")
                        if e < 2:
                            copy(PTS[:, 8 * e:8 * e + 8, :], ps[:, 6 + e, :].rearrange("p (k n) -> p k n", n=64)).then_inc(sh["st_kept"], 1)
                        else:
                            copy(PTS[:, 16:20, :], ps[:, 6, 0:256].rearrange("p (k n) -> p k n", n=64))
                            copy(PTS[0:DS, 20:22, :], ps[0:DS, 6, 256:384].rearrange("p (k n) -> p k n", n=64))
                            copy(PTS[0:NCS, 22, :], ps[0:NCS, 6, 384:448]).then_inc(sh["st_kept"], 1)
                    wait("pv_done")
                    for h in range(2):
                        hp = slice(HD * h, HD * (h + 1))
                        ins = copy(catT[hp, 0:G, ds(SEQ + b * DS, DS)], ps[hp, 4, h * 32:(h + 1) * 32].rearrange("p (g i) -> p g i", g=G))
                    ins.then_inc(sh["s_kept"], 1)
                    for n in per:
                        T[n].leave(DB)
                wait("x_upd", 8)
                act.wait_ge(sh["sq_summed"], T["sq_summed"].now())
                for k in range(KD):
                    square(k, KD, sq2, xT[:, k, :])
                root(nrs)
                wait("gb_zero")
                T["unit_made"].next(8)
                with act.Fori(0, FT // 2) as i:
                    for n, k in (("unit_made", 4), ("fs_saved", 2), ("act_done", 2), ("gc_done", 2)):
                        T[n].enter(i, k)
                    for s in range(2):
                        wait("unit_made")
                        wait("fs_saved", less=2)
                        wait("act_done", less=2)
                        gb, b0 = GBf[s], 4 * s
                        copy(gb[:, FW - 1:FW - 1 + HN], ps[:, b0, 0:HN])
                        copy(gb[:, FW - 1 + HN:FS0], ps[:, b0 + 1, 0:SEQ - HN])
                        seg = gb[:, FS0:FWD].rearrange("p (b n) -> p b n", b=DB)
                        hist = FP[:, ds((i * 2 + s) * 20 + 4, 16)].rearrange("p (b n) -> p b n", b=DB)
                        copy(seg[:, :, 0:FW - 1], hist)
                        copy(seg[:, :, FW - 1:FSEG], ps[:, b0 + 1, SEQ - HN:HN].rearrange("p (b n) -> p b n", b=DB)).then_inc(sh["gb_ready"], 1)
                        act.wait_ge(sh["gb_ready"], l * 22 + i * 2 + s + 1)
                        act.sem_inc(sh["ff_kept"], 1)
                        wait("unit_made")
                        copy(halves(upf[s]), ps[:, b0 + 2:b0 + 4, 0:HN]).then_inc(sh["ff_kept"], 1)
                        wait("gc_done")
                        act.activation(thf[s][:, 0:FO_W], gcf[s][:, 0:FO_W], ACT.Tanh, scale=0.5).then_inc(sh["ff_tanh"], 1)
                    for n in ("unit_made", "fs_saved", "act_done", "gc_done"):
                        T[n].leave(FT // 2)
                for e in range(6):
                    wait("fo_made")
                    w = min(4, FT - 4 * e) * P
                    copy(FO[:, 512 * e:512 * e + w], ps[0:18, 4 + e % 4, 0:w]).then_inc(sh["fo_kept"], 1)
            for t, m in TT:
                for hf in range(2):
                    n = 2 * t + hf
                    act.wait_ge(sh["y_made"], n + 1)
                    copy(xin[0:m, t, hf * 512:(hf + 1) * 512], ps[0:m, n % 8, :]).then_inc(sh["y_kept"], 1)

        @block.vector
        def _(dve):
            tt, ts, stt = dve.tensor_tensor, dve.tensor_scalar, dve.scalar_tensor_tensor
            dve.wait_ge(sh["const_in"], 16 * 19)
            dve.wait_ge(sh["const_ok"], 3)
            ts(idx[:, 0:DB], pgi[:, :], float(PAGE // CHUNK), sub[:, :], ALU.mult, ALU.add).then_inc(sh["setup_step"], 1)
            dve.memset(MX[:, P:P + 32], 0.0).then_inc(sh["setup_step"], 1)
            dve.tensor_copy(lower[:, :], lowf).then_inc(sh["setup_step"], 1)
            dve.wait_ge(sh["setup_step"], 3)
            ts(idx[:, DB:2 * DB], idx[:, 0:DB], float(NPOOL * PAGE // CHUNK), None, ALU.add).then_inc(sh["idx_made"], 1)
            for name, (_, credit) in PER.items():
                if credit and name != "layer_done":
                    dve.sem_inc(sh[name], credit)
            with dve.Fori(0, DEPTH) as l:
                T, wait = counters(dve, l)

                def step(ins):
                    ins.then_inc(sh["dve_step"], 1)
                    wait("dve_step")

                dve.wait_ge(sh["layer_done"], l + 1)
                wait("par_kept", 4)

                def rstd(bank, width, out):
                    ts(halves(out), ps[:, bank:bank + 2, 0:HN], 1.0 / width, EPS, ALU.mult, ALU.add).then_inc(sh["var_made"], 1)
                    wait("std_made")
                    step(dve.reciprocal(out, out))

                def norm(which):
                    wait("sq_summed", KD)
                    rstd(4, DM, nrs)
                    for k in range(KD):
                        stt(hT[:, k, :], xT[:, k, :], PV[:, 8 * which + k:8 * which + k + 1], nrs, ALU.mult, ALU.mult).then_inc(sh["h_made"], 1)

                norm(0)
                alone(dve)
                with dve.Fori(0, 2) as i:
                    T["dve_step"].enter(i, 2)
                    T["glu_gate"].enter(i, 2)
                    for q in range(2):
                        wait("glu_gate")
                        step(ts(gth[q], gth[q], 0.5, 0.5, ALU.mult, ALU.add))
                        xc = XC[:, ds(i * 2 + q, 1), :].rearrange("p a n -> p (a n)")
                        b0 = 4 * q
                        tt(xc[:, CW - 1:CW - 1 + HN], gth[q][:, 0:HN], ps[:, b0, 0:HN], ALU.mult)
                        tt(xc[:, CW - 1 + HN:XS0], gth[q][:, HN:SEQ], ps[:, b0 + 1, 0:SEQ - HN], ALU.mult)
                        tt(xc[:, XS0:XW].rearrange("p (b n) -> p b n", b=DB)[:, :, CW - 1:XSEG],
                           gth[q][:, SEQ:NT].rearrange("p (b n) -> p b n", b=DB),
                           ps[:, b0 + 1, SEQ - HN:HN].rearrange("p (b n) -> p b n", b=DB), ALU.mult).then_inc(sh["glu_done"], 1)
                    T["dve_step"].leave(2)
                    T["glu_gate"].leave(2)
                dve.wait_ge(sh["glu_done"], l * 4 + 6)
                wait("xz_made")
                alone(dve)
                with dve.Fori(0, CT - 1) as c:
                    T["dve_step"].enter(c, CW - 1)
                    xc = XC[:, ds(c, 1), :].rearrange("p a n -> p (a n)")
                    yc = catT[:, ds(CT + c, 1), :].rearrange("p a n -> p (a n)")
                    xs = xc[:, XS0:XW].rearrange("p (b n) -> p b n", b=DB)
                    ys = yc[:, SEQ:NT].rearrange("p (b n) -> p b n", b=DB)
                    for k in range(CW):
                        w = PV[:, ds(16 + 34 * c + k, 1)]
                        if k == 0:
                            bias = PV[:, ds(16 + 34 * c + CW, 1)]
                            ts(yc[:, 0:SEQ], xc[:, 0:SEQ], w, bias, ALU.mult, ALU.add)
                            ins = ts(ys, xs[:, :, 0:DS], w, bias, ALU.mult, ALU.add)
                        else:
                            stt(yc[:, 0:SEQ], xc[:, k:k + SEQ], w, yc[:, 0:SEQ], ALU.mult, ALU.add)
                            ins = stt(ys, xs[:, :, k:k + DS], w, ys, ALU.mult, ALU.add)
                        if k < CW - 1:
                            step(ins)
                    ins.then_inc(sh["conv_made"], 1)
                    T["dve_step"].leave(CT - 1)

                def head_means(t):
                    m = TT[t][1]
                    wait("head_sq")
                    ms = MS[0:m, 14 * t:14 * t + 14]
                    step(dve.tensor_reduce(ms, SQ[t % 2][0:m, :].rearrange("p (h d) -> p h d", h=14), X, ALU.add))
                    ts(ms, ms, 1.0 / HD, EPS, ALU.mult, ALU.add).then_inc(sh["head_ms"], 1)

                def heads(t):
                    m = TT[t][1]
                    zt = Z[0:m, t, :]
                    gates = zt[:, GB0:GB0 + 24]
                    step(ts(gates, gates, 0.5, 0.5, ALU.mult, ALU.add))
                    if t < 4:
                        g0 = gates.rearrange("p (k r) -> p k r", r=3)[:, :, 0]
                        ts(g0, g0, seen[0:m, t:t + 1], None, ALU.mult)
                    wait("head_rs")
                    zq = zt[:, 0:KVB].rearrange("p (h d) -> p h d", h=8)
                    zk = zt[:, KVB:KVB + 6 * P].rearrange("p (j x h d) -> p j x h d", j=3, x=2, h=2)[:, :, 0]
                    y, r1, r2 = SQ[t % 2][0:m, :], R1[0:m, :], R2[0:m, :]
                    yq = y[:, 0:512].rearrange("p (h d) -> p h d", h=8)
                    yk = y[:, 512:896].rearrange("p (j h d) -> p j h d", j=3, h=2)
                    rq = RS[0:m, 14 * t:14 * t + 8].unsqueeze(2).to_broadcast([m, 8, HD])
                    rk = RS[0:m, 14 * t + 8:14 * t + 14].rearrange("p (j h) -> p j h", j=3).unsqueeze(3).to_broadcast([m, 3, 2, HD])
                    tt(yq, zq, rq, ALU.mult)
                    step(tt(yk, zk, rk, ALU.mult))
                    tt(yq, yq, Gn[0:m, 0:HD].unsqueeze(1).to_broadcast([m, 8, HD]), ALU.mult)
                    step(tt(yk, yk, Gn[0:m, HD:4 * HD].rearrange("p (j d) -> p j d", j=3).unsqueeze(2).to_broadcast([m, 3, 2, HD]), ALU.mult))
                    cos = rope[0:m, t * HD:t * HD + 32].unsqueeze(1)
                    sin = rope[0:m, t * HD + 32:t * HD + 64].unsqueeze(1)
                    v = y.rearrange("p (h s d) -> p h s d", h=14, s=2)
                    v1 = r1.rearrange("p (h s d) -> p h s d", h=14, s=2)
                    v2 = r2.rearrange("p (h s d) -> p h s d", h=14, s=2)
                    tt(r1.rearrange("p (a d) -> p a d", a=28), y.rearrange("p (a d) -> p a d", a=28), cos.to_broadcast([m, 28, 32]), ALU.mult)
                    tt(v2[:, :, 0], v[:, :, 1], sin.to_broadcast([m, 14, 32]), ALU.mult)
                    step(tt(v2[:, :, 1], v[:, :, 0], sin.to_broadcast([m, 14, 32]), ALU.mult))
                    for s, op in ((0, ALU.subtract), (1, ALU.add)):
                        tt(zt[:, 0:KVB].rearrange("p (g h d) -> p h g d", g=G, h=2)[:, :, :, 32 * s:32 * s + 32],
                           v1[:, 0:8, s].rearrange("p (h g) d -> p h g d", h=2), v2[:, 0:8, s].rearrange("p (h g) d -> p h g d", h=2), op)
                        ins = tt(zk[:, :, :, 32 * s:32 * s + 32],
                                 v1[:, 8:14, s].rearrange("p (j h) d -> p j h d", j=3), v2[:, 8:14, s].rearrange("p (j h) d -> p j h d", j=3), op)
                    ins.then_inc(sh["qk_done"], 1)

                head_means(0)
                head_means(1)
                heads(0)
                head_means(2)
                heads(1)
                wait("mu_made")
                step(ts(halves(lnmu), ps[:, 5:7, 0:HN], 1.0 / CC, None, ALU.mult))
                for c in range(CT):
                    tt(catT[:, CT + c, :], catT[:, CT + c, :], lnmu, ALU.subtract).then_inc(sh["mu_taken"], 1)
                head_means(3)
                heads(2)
                wait("sq_summed", CT)
                rstd(5, CC, lnrs)
                head_means(4)
                heads(3)
                heads(4)
                for c in range(CT):
                    y = catT[:, CT + c, :]
                    step(tt(y, y, lnrs, ALU.mult))
                    ts(y, y, PV[:, 16 + 34 * c + 32:16 + 34 * c + 33], PV[:, 16 + 34 * c + 33:16 + 34 * c + 34], ALU.mult, ALU.add).then_inc(sh["ln_made"], 1)

                def gelu_in(n, nb, first=False):
                    wait("hid_made")
                    x, g = CX[:, 0:2 * nb], CG[:, 0:2 * nb]
                    step(ts(x, ps[:, 4, 0:2 * nb], posb[:, n:n + 1], None, ALU.add))
                    if n or not first:
                        dve.wait_ge(sh["cmp_out"], T["cmp_out"].now() + n)
                    step(stt(g, x, 0.044715, x, ALU.mult, ALU.mult))
                    stt(g, g, 1.0, x, ALU.add, ALU.mult).then_inc(sh["cmp_in"], 1)

                def gelu_out(nb):
                    x, g = CX[:, 0:2 * nb], CG[:, 0:2 * nb]
                    dve.wait_ge(sh["cmp_in"], T["cmp_in"].next())
                    step(ts(x, x, 0.5, None, ALU.mult))
                    wait("cmp_th")
                    stt(g, g, 1.0, x, ALU.add, ALU.mult).then_inc(sh["cmp_g"], 1)

                def compress(nb, first=False):
                    gelu_in(0, nb, first)
                    gelu_out(nb)
                    wait("kn_sq")
                    kn = KN[0:nb, :].rearrange("p (h d) -> p h d", h=2)
                    step(dve.tensor_reduce(KM[0:nb, 0:2], kn, X, ALU.add))
                    ts(KM[0:nb, 0:2], KM[0:nb, 0:2], 1.0 / HD, EPS, ALU.mult, ALU.add).then_inc(sh["kn_ms"], 1)
                    dve.wait_ge(sh["cmp_g"], T["cmp_g"].next())
                    wait("kn_rs")
                    step(tt(kn, ps[0:nb, 5, 0:P].rearrange("p (h d) -> p h d", h=2), KM[0:nb, 2:4].unsqueeze(2).to_broadcast([nb, 2, HD]), ALU.mult))
                    tt(kn, kn, kcg[0:nb, :].unsqueeze(1).to_broadcast([nb, 2, HD]), ALU.mult).then_inc(sh["kn_made"], 1)
                    gelu_in(1, nb)
                    gelu_out(nb)
                    T["cmp_g"].next()
                    T["cmp_out"].next(2)

                wait("posb_kept")
                compress(NCP, True)
                wait("tr_kept", 10)
                dve.wait_ge(sh["hid_made"], T["hid_made"].now())
                alone(dve)
                with dve.Fori(0, G) as g:
                    per = dict(sc_made=8, pt_made=24, exped=8, dve_step=PU_STEPS)
                    for n, k in per.items():
                        T[n].enter(g, k)
                    dve.wait_ge(sh["sc_made"], T["sc_made"].now())
                    dve.tensor_copy(QG, QT[:, ds(g, 1), 0:SEQ].rearrange("p a n -> p (a n)")).then_inc(sh["qg_made"], 1)

                    def mask(u):
                        t, c, pb = u % 4, 16 * (u % 2), PB[u % 2]
                        wait("sc_made")
                        wait("pt_made", 3, less=6)
                        alone(dve)
                        n = (t + 1) * P
                        dve.tensor_tensor_reduce(pb[:, 1024:1024 + NCP], ps[:, 4, 64 * (u % 2):64 * (u % 2) + NCP], cmpm[:, t * NCP:(t + 1) * NCP],
                                                 1.0, -3.0e38, ALU.add, ALU.max, st[:, c:c + 1])
                        for e in range(2):
                            ins = dve.tensor_tensor_reduce(pb[:, 512 * e:512 * e + n], ps[:, 2 * e + u % 2, 0:n], causal[:, SEQ - n:SEQ],
                                                           1.0, -3.0e38, ALU.add, ALU.max, st[:, c + 1 + e:c + 2 + e])
                        step(ins)
                        ts(st[:, c + 3:c + 6], st[:, c:c + 3], -SCALE, None, ALU.mult).then_inc(sh["masked"], 1)

                    def weight(u):
                        h, t, c, pb = u // 4, u % 4, 16 * (u % 2), PB[u % 2]
                        wait("exped")
                        r = st[:, c + 6:c + 9]
                        step(ts(r, r, 1e-30, None, ALU.max))
                        step(dve.reciprocal(r, r))
                        step(tt(r, r, Z[:, t, ds(GB0 + 12 * h + 3 * g, 3)], ALU.mult))
                        n = (t + 1) * P
                        for e, (o, w) in enumerate(((1024, NCP), (0, n), (512, n))):
                            ins = ts(pb[:, o:o + w], pb[:, o:o + w], st[:, c + 6 + e:c + 7 + e], None, ALU.mult)
                        ins.then_inc(sh["p_ready"], 1)

                    mask(0)
                    for u in range(8):
                        weight(u)
                        if u < 7:
                            mask(u + 1)
                    for n in per:
                        T[n].leave(G)
                dve.wait_ge(sh["ln_made"], T["ln_made"].next(4))
                for c in range(CT):
                    y = catT[:, CT + c, :]
                    wait("ln_tanh")
                    step(ts(thl[c % 2], thl[c % 2], 0.5, 0.5, ALU.mult, ALU.add))
                    tt(y, y, thl[c % 2], ALU.mult).then_inc(sh["conv_done"], 1)
                wait("gates_in", 128)
                alone(dve)
                with dve.Fori(0, DB) as b:
                    per = dict(hid_made=2, cmp_in=2, cmp_out=2, cmp_th=2, kn_sq=1, kn_rs=1, cmp_g=2, win_made=1, small_made=1, cmp_exp=1,
                               imp_made=1, slc_made=1, s_exped=1, dve_step=SB_STEPS)
                    for n, k in per.items():
                        T[n].enter(b, k)
                    dve.wait_ge(sh["win_made"], T["win_made"].now())
                    for h in range(2):
                        hp = slice(HD * h, HD * (h + 1))
                        ins = dve.tensor_copy(QBs[hp, 32 * h:32 * h + 32].rearrange("p (g i) -> p g i", g=G), QT[hp, :, ds(SEQ + b * DS, DS)])
                    ins.then_inc(sh["qb_made"], 1)
                    compress(NCS)
                    s = st[0:64]
                    wait("small_made")
                    step(dve.tensor_reduce(s[:, 0:1], ps[0:64, 5, 16:16 + NCS], X, ALU.max))
                    ts(s[:, 1:2], s[:, 0:1], -SCALE, None, ALU.mult).then_inc(sh["cmp_max"], 1)
                    wait("cmp_exp")
                    step(ts(s[:, 3:4], s[:, 2:3], 1e-30, None, ALU.max))
                    step(dve.reciprocal(s[:, 3:4], s[:, 3:4]))
                    sc = S[:, 2576:2576 + NCS]
                    ts(sc, sc, s[:, 3:4], None, ALU.mult).then_inc(sh["pc_ready"], 1)
                    wait("win_made")
                    alone(dve)
                    for o, w, src, m, c in ((2048, DS, ps[0:64, 5, 0:DS], newm, 8), (2056, WIN, ps[0:64, 7, :], winm, 9),
                                            (2568, DS, ps[0:64, 5, DS:2 * DS], newm, 10)):
                        ins = dve.tensor_tensor_reduce(S[:, o:o + w], src, m[:, :], 1.0, -3.0e38, ALU.add, ALU.max, s[:, c:c + 1])
                    step(ins)
                    step(dve.tensor_reduce(s[:, 13:14], s[:, 9:11], X, ALU.max))
                    ts(s[:, 15:16], s[:, 13:14], -SCALE, None, ALU.mult).then_inc(sh["w_masked"], 1)
                    wait("imp_made")
                    step(dve.tensor_copy(impv[:, 0:NCAND], ps[0:64, 4, 0:NCAND]))
                    nn = [64, NCAND, NCAND]
                    vi = impv[:, 0:NCAND].unsqueeze(2).to_broadcast(nn)
                    vj = impv[:, 0:NCAND].unsqueeze(1).to_broadcast(nn)
                    gt = S[:, 0:900].rearrange("p (i j) -> p i j", i=NCAND)
                    eq = S[:, 900:1800].rearrange("p (i j) -> p i j", i=NCAND)
                    tt(gt, vj, vi, ALU.is_gt)
                    step(tt(eq, vj, vi, ALU.is_equal))
                    step(tt(S[:, 900:1800], S[:, 900:1800], lower[:, :], ALU.mult))
                    step(tt(S[:, 0:900], S[:, 0:900], S[:, 900:1800], ALU.add))
                    step(dve.tensor_reduce(impv[:, NCAND:2 * NCAND], gt, X, ALU.add))
                    step(ts(MX[:, P + 1:P + 1 + NCAND], impv[:, NCAND:2 * NCAND], NPICK - 0.5, NEG, ALU.is_gt, ALU.mult))
                    step(dve.tensor_copy(MX[:, 0:P].rearrange("p (n e) -> p n e", e=4), MX[:, P:P + 32].unsqueeze(2).to_broadcast([64, 32, 4])))
                    wait("slc_made")
                    alone(dve)
                    for n in range(4):
                        ins = dve.tensor_tensor_reduce(S[:, n * 512:(n + 1) * 512].rearrange("p (j n) -> p j n", j=4),
                                                       ps[0:64, n, :].rearrange("p (j n) -> p j n", j=4),
                                                       MX[:, 0:P].unsqueeze(1).to_broadcast([64, 4, P]),
                                                       1.0, -3.0e38, ALU.add, ALU.max, s[:, 4 + n:5 + n])
                    step(ins)
                    step(dve.tensor_reduce(s[:, 12:13], s[:, 4:9], X, ALU.max))
                    ts(s[:, 14:15], s[:, 12:13], -SCALE, None, ALU.mult).then_inc(sh["s_masked"], 1)
                    ts(sc, sc, GR[:, ds(b * 3, 1)], None, ALU.mult)
                    wait("s_exped")
                    step(ts(s[:, 16:18], s[:, 16:18], 1e-30, None, ALU.max))
                    step(dve.reciprocal(s[:, 16:18], s[:, 16:18]))
                    step(tt(s[:, 16:18], s[:, 16:18], GR[:, ds(b * 3 + 1, 2)], ALU.mult))
                    ts(S[:, 0:2056], S[:, 0:2056], s[:, 16:17], None, ALU.mult)
                    ts(S[:, 2056:2576], S[:, 2056:2576], s[:, 17:18], None, ALU.mult).then_inc(sh["s_ready"], 1)
                    for n in per:
                        T[n].leave(DB)
                T["unit_made"].next(8)
                alone(dve)
                with dve.Fori(0, 2) as i:
                    T["unit_made"].enter(i, 4)
                    for s in range(4):
                        wait("unit_made")
                        xm = xT[:, ds(i * 4 + s, 1), :].rearrange("p a (h n) -> p (a h) n", h=2)
                        tt(xm, xm, ps[:, 2 * s:2 * s + 2, 0:HN], ALU.add).then_inc(sh["x_upd"], 1)
                    T["unit_made"].leave(2)
                norm(1)
                wait("kv_out", 16 * 12)
                alone(dve)
                with dve.Fori(0, FT // 2) as i:
                    for n, k in (("gb_ready", 2), ("ff_tanh", 2), ("ff_kept", 4), ("dve_step", FF_STEPS)):
                        T[n].enter(i, k)
                    for s in range(2):
                        wait("gb_ready")
                        gb, gc, th, up = GBf[s], gcf[s][:, 0:FO_W], thf[s][:, 0:FO_W], upf[s]

                        def w(k):
                            return FP[:, ds((i * 2 + s) * 20 + k, 1)]

                        step(ts(gc, gb[:, 0:FO_W], w(0), w(3), ALU.mult, ALU.add))
                        step(stt(gc, gb[:, 1:1 + FO_W], w(1), gc, ALU.mult, ALU.add))
                        stt(gc, gb[:, 2:2 + FO_W], w(2), gc, ALU.mult, ALU.add).then_inc(sh["gc_done"], 1)
                        wait("ff_tanh")
                        step(stt(th, th, 1.0, gc, ALU.add, ALU.mult))
                        wait("ff_kept", 2)
                        af = actT[:, ds(i * 2 + s, 1), :].rearrange("p a n -> p (a n)")
                        stt(af[:, 0:SEQ], th[:, 0:SEQ], 0.5, up[:, 0:SEQ], ALU.mult, ALU.mult)
                        seg = thf[s][:, FS0:FWD].rearrange("p (b n) -> p b n", b=DB)[:, :, 0:DS]
                        stt(af[:, SEQ:NT].rearrange("p (b n) -> p b n", b=DB), seg, 0.5,
                            up[:, SEQ:NT].rearrange("p (b n) -> p b n", b=DB), ALU.mult, ALU.mult).then_inc(sh["act_done"], 1)
                    for n in ("gb_ready", "ff_tanh", "ff_kept", "dve_step"):
                        T[n].leave(FT // 2)
                alone(dve)
                with dve.Fori(0, 4) as i:
                    T["down_made"].enter(i, 2)
                    for s in range(2):
                        wait("down_made")
                        xm = xT[:, ds(i * 2 + s, 1), :].rearrange("p a (h n) -> p (a h) n", h=2)
                        tt(xm, xm, ps[:, 2 * s:2 * s + 2, 0:HN], ALU.add).then_inc(sh["x_upd"], 1)
                    T["down_made"].leave(4)
                dve.wait_ge(sh["x_upd"], l * 16 + 20)
                wait("fo_out", 32)
                dve.wait_ge(sh["u_out"], l * 32 + 32)
                dve.sem_inc(sh["layer_done"], 1)
                T["dve_step"].end()



INS = ["x_prompt", "x_sample", "cache_k_cmp", "cache_v_cmp", "cache_k_slc", "cache_v_slc", "state_k_win", "state_v_win",
       "state_conv", "state_ffn_conv", "page_table", "attn_norm", "w_in", "q_norm", "k_norm", "kc_norm", "cmp_pos",
       "cmp_w1_k", "cmp_w2_k", "cmp_w1_v", "cmp_w2_v", "conv_w", "conv_b", "conv_ln_g", "conv_ln_b", "w_out",
       "ffn_norm", "w_up", "ffn_conv_w", "ffn_conv_b", "w_down"]
PK, SK, SW = (DEPTH, 1, SEQ, NKV, HD), (DEPTH, DB, DS, NKV, HD), (DEPTH, DB, WIN, NKV, HD)
OUTS = [("y_prompt", (1, SEQ, DM)), ("y_sample", (DB, DS, DM)), ("p_k_cmp", PK), ("p_v_cmp", PK), ("p_k_slc", PK),
        ("p_v_slc", PK), ("p_k_win", PK), ("p_v_win", PK), ("p_conv", (DEPTH, 1, CW - 1, CC)),
        ("p_ffn_conv", (DEPTH, 1, FW - 1, DFF)), ("s_k_cmp", SK), ("s_v_cmp", SK), ("s_k_slc", SK), ("s_v_slc", SK),
        ("s_k_win", SW), ("s_v_win", SW), ("s_conv", (DEPTH, DB, CW - 1, CC)), ("s_ffn_conv", (DEPTH, DB, FW - 1, DFF))]


def kernel(**inputs):
    from concourse.bacc import Bacc
    from concourse.bass_utils import run_bass_kernel_spmd

    nc = Bacc("TRN2", target_bir_lowering=False, num_devices=1)
    arrays, I, O = {}, {}, {}
    for name, a in list(host_tables().items()) + [(n, inputs[n]) for n in INS]:
        a = np.ascontiguousarray(a)
        arrays["in_" + name] = a
        I[name] = nc.dram_tensor("in_" + name, a.shape, mybir.dt.from_np(a.dtype), kind="ExternalInput").ap()
    for name, shape in OUTS:
        O[name] = nc.dram_tensor("out_" + name, shape, F32, kind="ExternalOutput").ap()
    build(nc, I, O)
    r = run_bass_kernel_spmd(nc, [arrays], core_ids=[0])
    return tuple(r.results[0]["out_" + name] for name, _ in OUTS)
```
